# Optimizing a Trainium2 kernel written in Bass

```python
import jax, jax.numpy as jnp
from jax import lax
import numpy as np
import math

D_MODEL = 1024
BATCH = 1
SEQ = 1024
DEPTH = 1

CHUNK = 64
Q_BLOCK = 128
HEAD_DIM = 64
N_HEADS_FOX = 8
N_HEADS_DSA = 8
IDX_HEADS = 8
IDX_DIM = 64
TOPK_MAX = 256
ROPE_THETA = 10000.0
N_GROUPS = 4
EXPERTS_PER_GROUP = 8
N_EXPERTS = N_GROUPS * EXPERTS_PER_GROUP
TOP_K_INNER = 2
D_EXPERT = 512
EPS = 1e-6

W_FOX = N_HEADS_FOX * HEAD_DIM
W_DSA = N_HEADS_DSA * HEAD_DIM
IN_SPLITS = (W_FOX, W_FOX, W_FOX, N_HEADS_FOX,
             W_DSA, HEAD_DIM, HEAD_DIM,
             IDX_HEADS * IDX_DIM, IDX_DIM, IDX_HEADS,
             D_MODEL, D_MODEL)
IN_COLS = 3 * W_FOX + N_HEADS_FOX + W_DSA + 2 * HEAD_DIM + IDX_HEADS * IDX_DIM + IDX_DIM + IDX_HEADS + 2 * D_MODEL


def rmsnorm(x, g):
    xf = x.astype(jnp.float32)
    y = xf * lax.rsqrt(jnp.mean(xf * xf, axis=-1, keepdims=True) + EPS)
    return (y * g.astype(jnp.float32)).astype(x.dtype)

def rope(x, pos):
    half = x.shape[-1] // 2
    inv = ROPE_THETA ** (-jnp.arange(half, dtype=jnp.float32) / half)
    ang = pos.astype(jnp.float32)[..., None] * inv
    cos = jnp.cos(ang)[:, :, None, :]
    sin = jnp.sin(ang)[:, :, None, :]
    x1 = x[..., :half].astype(jnp.float32)
    x2 = x[..., half:].astype(jnp.float32)
    out = jnp.concatenate([x1 * cos - x2 * sin, x2 * cos + x1 * sin], axis=-1)
    return out.astype(x.dtype)

def forgetting_attention(q, k, v, log_f):
    B, S, H, D = q.shape
    Ft = jnp.cumsum(log_f, axis=1).transpose(0, 2, 1)
    scale = D ** -0.5
    outs = []
    for start in range(0, S, Q_BLOCK):
        end = start + Q_BLOCK
        s = jnp.einsum('bqhd,bkhd->bhqk', q[:, start:end], k[:, :end],
                       preferred_element_type=jnp.float32) * scale
        s = s + Ft[:, :, start:end, None] - Ft[:, :, None, :end]
        tq = jnp.arange(start, end)[:, None]
        tk = jnp.arange(end)[None, :]
        s = jnp.where(tk <= tq, s, -jnp.inf)
        p = jax.nn.softmax(s, axis=-1)
        outs.append(jnp.einsum('bhqk,bkhd->bqhd', p.astype(v.dtype), v[:, :end]))
    return jnp.concatenate(outs, axis=1)

def dsa_attention(q, k, v, qi, ki, wi):
    B, S, H, D = q.shape
    topk = min(TOPK_MAX, S // 4)
    chunk_id = jnp.arange(S) // CHUNK
    scale = D ** -0.5
    gather = jax.vmap(lambda arr, ids: arr[ids])
    outs = []
    for start in range(0, S, Q_BLOCK):
        end = start + Q_BLOCK
        kk = min(topk, end)
        dots = jnp.einsum('bqhd,bkd->bqhk', qi[:, start:end], ki[:, :end],
                          preferred_element_type=jnp.float32)
        score = jnp.einsum('bqh,bqhk->bqk', wi[:, start:end].astype(jnp.float32), jax.nn.relu(dots))
        cq = chunk_id[start:end]
        allowed = chunk_id[:end][None, :] <= cq[:, None]
        score = jnp.where(allowed[None], score, -jnp.inf)
        _, idx = lax.top_k(score, kk)
        valid = chunk_id[idx] <= cq[None, :, None]
        kg = gather(k[:, :end], idx)
        vg = gather(v[:, :end], idx)
        s = jnp.einsum('bqhd,bqkd->bhqk', q[:, start:end], kg,
                       preferred_element_type=jnp.float32) * scale
        s = jnp.where(valid[:, None], s, -jnp.inf)
        p = jax.nn.softmax(s, axis=-1)
        outs.append(jnp.einsum('bhqk,bqkd->bqhd', p.astype(vg.dtype), vg))
    return jnp.concatenate(outs, axis=1)

def hierarchical_moe(h, w_grp, b_grp, w_exp, b_exp, w1, w3, w2):
    N, D = h.shape
    g_logits = jnp.matmul(h, w_grp).astype(jnp.float32) + b_grp.astype(jnp.float32)
    g_prob = jax.nn.softmax(g_logits, axis=-1)
    g_idx = jnp.argmax(g_logits, axis=-1)
    g_w = jnp.take_along_axis(g_prob, g_idx[:, None], axis=1)[:, 0]
    e_logits = (jnp.matmul(h, w_exp).astype(jnp.float32) + b_exp.astype(jnp.float32))
    e_logits = e_logits.reshape(N, N_GROUPS, EXPERTS_PER_GROUP)
    e_logits = jnp.take_along_axis(e_logits, g_idx[:, None, None], axis=1)[:, 0]
    e_prob = jax.nn.softmax(e_logits, axis=-1)
    top_p, top_local = lax.top_k(e_prob, TOP_K_INNER)
    top_p = top_p / jnp.sum(top_p, axis=-1, keepdims=True)
    weights = (g_w[:, None] * top_p).reshape(-1)
    expert = (g_idx[:, None] * EXPERTS_PER_GROUP + top_local).reshape(-1)
    order = jnp.argsort(expert)
    tok = order // TOP_K_INNER
    xs = h[tok]
    sizes = jnp.bincount(expert, length=N_EXPERTS).astype(jnp.int32)
    a = lax.ragged_dot(xs, w1, sizes)
    b = lax.ragged_dot(xs, w3, sizes)
    y = lax.ragged_dot(jax.nn.silu(a) * b, w2, sizes)
    y = (y * weights[order][:, None]).astype(h.dtype)
    return jax.ops.segment_sum(y, tok, num_segments=N)

def first_inputs(seed: int = 0) -> dict:
    key = jax.random.key(seed)
    ks = jax.random.split(key, 24)
    f32 = jnp.float32
    nrm = lambda k, shape, fan: jax.random.normal(k, shape, f32) * fan ** -0.5
    L = DEPTH
    x = jax.random.normal(ks[0], (BATCH, SEQ, D_MODEL), f32)
    c = jax.random.normal(ks[1], (BATCH, D_MODEL), f32)
    offsets = jax.random.randint(ks[2], (BATCH,), 0, 64) * CHUNK
    positions = (offsets[:, None] + jnp.arange(SEQ)[None, :]).astype(jnp.int32)
    return {
        'x': x,
        'c': c,
        'positions': positions,
        'ada_w': nrm(ks[3], (L, D_MODEL, 6 * D_MODEL), D_MODEL) * 0.5,
        'ada_b': jax.random.normal(ks[4], (L, 6 * D_MODEL), f32) * 0.02,
        'norm1_g': 1.0 + 0.05 * jax.random.normal(ks[5], (L, D_MODEL), f32),
        'norm2_g': 1.0 + 0.05 * jax.random.normal(ks[6], (L, D_MODEL), f32),
        'w_in': nrm(ks[7], (L, D_MODEL, IN_COLS), D_MODEL),
        'b_fgt': jax.random.uniform(ks[8], (L, N_HEADS_FOX), f32, 1.0, 4.0),
        'b_gate': jax.random.normal(ks[9], (L, 2 * D_MODEL), f32) * 0.02,
        'qn_fox': 1.0 + 0.05 * jax.random.normal(ks[10], (L, HEAD_DIM), f32),
        'kn_fox': 1.0 + 0.05 * jax.random.normal(ks[11], (L, HEAD_DIM), f32),
        'qn_dsa': 1.0 + 0.05 * jax.random.normal(ks[12], (L, HEAD_DIM), f32),
        'kn_dsa': 1.0 + 0.05 * jax.random.normal(ks[13], (L, HEAD_DIM), f32),
        'w_proj_fox': nrm(ks[14], (L, W_FOX, D_MODEL), W_FOX),
        'w_proj_dsa': nrm(ks[15], (L, W_DSA, D_MODEL), W_DSA),
        'w_out': nrm(ks[16], (L, D_MODEL, D_MODEL), D_MODEL),
        'router_w_grp': nrm(ks[17], (L, D_MODEL, N_GROUPS), D_MODEL),
        'router_b_grp': jax.random.normal(ks[18], (L, N_GROUPS), f32) * 0.01,
        'router_w_exp': nrm(ks[19], (L, D_MODEL, N_EXPERTS), D_MODEL),
        'router_b_exp': jax.random.normal(ks[20], (L, N_EXPERTS), f32) * 0.01,
        'exp_w1': nrm(ks[21], (L, N_EXPERTS, D_MODEL, D_EXPERT), D_MODEL),
        'exp_w3': nrm(ks[22], (L, N_EXPERTS, D_MODEL, D_EXPERT), D_MODEL),
        'exp_w2': nrm(ks[23], (L, N_EXPERTS, D_EXPERT, D_MODEL), D_EXPERT),
    }

def first_block(x, c, positions, ada_w, ada_b, norm1_g, norm2_g, w_in, b_fgt, b_gate,
              qn_fox, kn_fox, qn_dsa, kn_dsa, w_proj_fox, w_proj_dsa, w_out,
              router_w_grp, router_b_grp, router_w_exp, router_b_exp,
              exp_w1, exp_w3, exp_w2):
    B, S, D = x.shape
    split_at = np.cumsum(IN_SPLITS)[:-1].tolist()
    c_act = jax.nn.silu(c)
    for l in range(DEPTH):
        mod = jnp.matmul(c_act, ada_w[l]) + ada_b[l]
        sh1, sc1, gt1, sh2, sc2, gt2 = [m[:, None, :] for m in jnp.split(mod, 6, axis=-1)]

        h = rmsnorm(x, norm1_g[l]) * (1.0 + sc1) + sh1
        proj = jnp.matmul(h, w_in[l])
        (fq, fk, fv, flog, dq, dk, dv, iq, ik, iw, g_fox, g_dsa) = jnp.split(proj, split_at, axis=-1)

        fq = rmsnorm(fq.reshape(B, S, N_HEADS_FOX, HEAD_DIM), qn_fox[l])
        fk = rmsnorm(fk.reshape(B, S, N_HEADS_FOX, HEAD_DIM), kn_fox[l])
        fv = fv.reshape(B, S, N_HEADS_FOX, HEAD_DIM)
        log_f = jax.nn.log_sigmoid((flog + b_fgt[l]).astype(jnp.float32))
        out_fox = forgetting_attention(fq, fk, fv, log_f).reshape(B, S, W_FOX)

        dq = rope(rmsnorm(dq.reshape(B, S, N_HEADS_DSA, HEAD_DIM), qn_dsa[l]), positions)
        dk = rope(rmsnorm(dk.reshape(B, S, 1, HEAD_DIM), kn_dsa[l]), positions)[:, :, 0]
        iq = rope(iq.reshape(B, S, IDX_HEADS, IDX_DIM), positions)
        ik = rope(ik.reshape(B, S, 1, IDX_DIM), positions)[:, :, 0]
        out_dsa = dsa_attention(dq, dk, dv, iq, ik, iw).reshape(B, S, W_DSA)

        merged = (jax.nn.sigmoid(g_fox + b_gate[l, :D]) * jnp.matmul(out_fox, w_proj_fox[l])
                  + jax.nn.sigmoid(g_dsa + b_gate[l, D:]) * jnp.matmul(out_dsa, w_proj_dsa[l]))
        x = x + gt1 * jnp.matmul(merged, w_out[l])

        h2 = rmsnorm(x, norm2_g[l]) * (1.0 + sc2) + sh2
        y = hierarchical_moe(h2.reshape(B * S, D), router_w_grp[l], router_b_grp[l],
                             router_w_exp[l], router_b_exp[l],
                             exp_w1[l], exp_w3[l], exp_w2[l]).reshape(B, S, D)
        x = x + gt2 * y
    return x


N_ATTN_HEADS = 8
N_DELTA_HEADS = 8
ATTN_WIDTH = N_ATTN_HEADS * HEAD_DIM
DELTA_WIDTH = N_DELTA_HEADS * HEAD_DIM
MIX_WIDTH = ATTN_WIDTH + DELTA_WIDTH
DILATED_BRANCHES = ((128, 1), (512, 4), (2048, 16))
PAD_UNIT = 2048
N_BUCKETS = 32
MAX_DISTANCE = 2048
CONV_WIDTH = 4
D_FF = (8 * D_MODEL + 3 * 256 - 1) // (3 * 256) * 256
IN_WIDTH = 3 * ATTN_WIDTH + 4 * DELTA_WIDTH + 2 * N_DELTA_HEADS
NEG_INF = -1e30


def _rmsnorm(x, g):
    x32 = x.astype(jnp.float32)
    y = x32 * lax.rsqrt(jnp.mean(x32 * x32, axis=-1, keepdims=True) + EPS)
    return (y * g.astype(jnp.float32)).astype(x.dtype)

def _l2norm(x):
    return x * lax.rsqrt(jnp.sum(x * x, axis=-1, keepdims=True) + EPS)

def _t5_bucket(distance):
    max_exact = N_BUCKETS // 2
    dist_f = jnp.maximum(distance, 1).astype(jnp.float32)
    large = max_exact + (jnp.log(dist_f / max_exact) / math.log(MAX_DISTANCE / max_exact)
                         * (N_BUCKETS - max_exact)).astype(jnp.int32)
    return jnp.where(distance < max_exact, distance, jnp.minimum(large, N_BUCKETS - 1))

def _dilated_branch(q, k, v, rel_bias, window, dilation):
    b, h, p, dh = q.shape
    band = window // dilation
    length = p // dilation
    n_blocks = length // band

    def to_blocks(t):
        t = t.reshape(b, h, length, dilation, dh).transpose(0, 1, 3, 2, 4)
        return t.reshape(b, h, dilation, n_blocks, band, dh)

    qb, kb, vb = to_blocks(q), to_blocks(k), to_blocks(v)

    def with_prev(t):
        prev = jnp.pad(t, ((0, 0), (0, 0), (0, 0), (1, 0), (0, 0), (0, 0)))[:, :, :, :-1]
        return jnp.concatenate([prev, t], axis=-2)

    kw, vw = with_prev(kb), with_prev(vb)
    qi = jnp.arange(band)[:, None]
    kj = jnp.arange(2 * band)[None, :]
    steps = qi + band - kj
    in_window = (steps >= 0) & (steps <= band)
    not_before_start = (jnp.arange(n_blocks)[:, None, None] > 0) | (kj >= band)[None]
    valid = in_window[None] & not_before_start
    bias = rel_bias.astype(jnp.float32)[_t5_bucket(jnp.maximum(steps, 0) * dilation)]
    bias = bias.transpose(2, 0, 1)
    s = jnp.einsum('bhrnqd,bhrnkd->bhrnqk', qb * dh ** -0.5, kw) + bias[None, :, None, None]
    s = jnp.where(valid, s, NEG_INF)
    m = jnp.max(s, axis=-1, keepdims=True)
    e = jnp.exp(s - m)
    denom = jnp.sum(e, axis=-1, keepdims=True)
    o = jnp.einsum('bhrnqk,bhrnkd->bhrnqd', e, vw) / denom
    lse = (m + jnp.log(denom))[..., 0]
    o = o.reshape(b, h, dilation, length, dh).transpose(0, 1, 3, 2, 4).reshape(b, h, p, dh)
    lse = lse.reshape(b, h, dilation, length).transpose(0, 1, 3, 2).reshape(b, h, p)
    return o, lse

def _dilated_attention(q, k, v, rel_bias):
    b, s, h, dh = q.shape
    p = (s + PAD_UNIT - 1) // PAD_UNIT * PAD_UNIT

    def to_bhpd(t):
        t = jnp.pad(t.astype(jnp.float32), ((0, 0), (0, p - s), (0, 0), (0, 0)))
        return t.transpose(0, 2, 1, 3)

    q, k, v = to_bhpd(q), to_bhpd(k), to_bhpd(v)
    outs, lses = [], []
    for window, dilation in DILATED_BRANCHES:
        o_i, lse_i = _dilated_branch(q, k, v, rel_bias, window, dilation)
        outs.append(o_i)
        lses.append(lse_i)
    w = jax.nn.softmax(jnp.stack(lses), axis=0)
    o = jnp.sum(w[..., None] * jnp.stack(outs), axis=0)
    return o[:, :, :s].transpose(0, 2, 1, 3).reshape(b, s, h * dh)

def _causal_conv(x, w):
    return lax.conv_general_dilated(x, w[:, None, :], window_strides=(1,),
                                    padding=((CONV_WIDTH - 1, 0),),
                                    dimension_numbers=('NWC', 'WIO', 'NWC'),
                                    feature_group_count=x.shape[-1])

def _chunk_gated_delta_rule(q, k, v, g, beta):
    b, s, h, dk = q.shape
    dv = v.shape[-1]
    nc = s // CHUNK

    def chunks(t):
        return t.reshape(b, nc, CHUNK, h, t.shape[-1]).transpose(1, 0, 3, 2, 4)

    qc, kc, vc = chunks(q), chunks(k), chunks(v)
    gcum = jnp.cumsum(g.reshape(b, nc, CHUNK, h).transpose(1, 0, 3, 2), axis=-1)
    bc = beta.reshape(b, nc, CHUNK, h).transpose(1, 0, 3, 2)
    causal = jnp.tril(jnp.ones((CHUNK, CHUNK), dtype=bool))
    strict = jnp.tril(jnp.ones((CHUNK, CHUNK), dtype=bool), k=-1)
    diff = gcum[..., :, None] - gcum[..., None, :]
    decay = jnp.where(causal, jnp.exp(jnp.where(causal, diff, 0.0)), 0.0)
    k_beta = kc * bc[..., None]
    a_mat = jnp.where(strict, jnp.einsum('nbhcd,nbhed->nbhce', k_beta, kc) * decay, 0.0)
    rhs = jnp.concatenate([vc * bc[..., None], k_beta * jnp.exp(gcum)[..., None]], axis=-1)
    sol = lax.linalg.triangular_solve(a_mat + jnp.eye(CHUNK, dtype=a_mat.dtype), rhs,
                                      left_side=True, lower=True, unit_diagonal=True)
    u, w = sol[..., :dv], sol[..., dv:]
    qk = jnp.where(causal, jnp.einsum('nbhcd,nbhed->nbhce', qc, kc) * decay, 0.0)

    def step(state, xs):
        q_i, k_i, u_i, w_i, g_i, qk_i = xs
        v_new = u_i - jnp.einsum('bhck,bhkv->bhcv', w_i, state)
        o_i = (jnp.einsum('bhck,bhkv->bhcv', q_i * jnp.exp(g_i)[..., None], state)
               + jnp.einsum('bhce,bhev->bhcv', qk_i, v_new))
        g_last = g_i[..., -1]
        k_dec = k_i * jnp.exp(g_last[..., None] - g_i)[..., None]
        state = state * jnp.exp(g_last)[..., None, None] + jnp.einsum('bhck,bhcv->bhkv', k_dec, v_new)
        return state, o_i

    state0 = jnp.zeros((b, h, dk, dv), jnp.float32)
    _, o = lax.scan(step, state0, (qc, kc, u, w, gcum, qk))
    return o.transpose(1, 0, 3, 2, 4).reshape(b, s, h, dv)

def _gated_deltanet(q, k, v, z, b_logit, a_logit, conv_w, a_log, dt_bias, norm_g):
    bsz, s, _ = q.shape
    qkv = jax.nn.silu(_causal_conv(jnp.concatenate([q, k, v], axis=-1), conv_w))
    q, k, v = jnp.split(qkv.astype(jnp.float32), 3, axis=-1)
    shp = (bsz, s, N_DELTA_HEADS, HEAD_DIM)
    q = _l2norm(q.reshape(shp)) * HEAD_DIM ** -0.5
    k = _l2norm(k.reshape(shp))
    v = v.reshape(shp)
    beta = jax.nn.sigmoid(b_logit.astype(jnp.float32))
    g = -jnp.exp(a_log.astype(jnp.float32)) * jax.nn.softplus(
        a_logit.astype(jnp.float32) + dt_bias.astype(jnp.float32))
    o = _chunk_gated_delta_rule(q, k, v, g, beta)
    o = _rmsnorm(o, norm_g) * jax.nn.silu(z.astype(jnp.float32).reshape(shp))
    return o.reshape(bsz, s, DELTA_WIDTH).astype(z.dtype)

def second_inputs(seed: int = 0) -> dict:
    key = jax.random.key(seed)
    ks = jax.random.split(key, 20)
    f32 = jnp.float32

    def nrm(k, shape, scale):
        return jax.random.normal(k, shape, f32) * scale

    dt = jnp.exp(jax.random.uniform(ks[9], (DEPTH, N_DELTA_HEADS), f32,
                                    minval=math.log(1e-3), maxval=math.log(1e-1)))
    return {
        'x': nrm(ks[0], (BATCH, SEQ, D_MODEL), 1.0),
        'c': nrm(ks[1], (BATCH, D_MODEL), 1.0),
        'w_ada': nrm(ks[2], (DEPTH, D_MODEL, 6 * D_MODEL), 0.5 * D_MODEL ** -0.5),
        'b_ada': nrm(ks[3], (DEPTH, 6 * D_MODEL), 0.02),
        'norm_attn_g': 1.0 + nrm(ks[4], (DEPTH, D_MODEL), 0.05),
        'w_in': nrm(ks[5], (DEPTH, D_MODEL, IN_WIDTH), D_MODEL ** -0.5),
        'rel_bias': nrm(ks[6], (N_BUCKETS, N_ATTN_HEADS), 0.5),
        'conv_w': nrm(ks[7], (DEPTH, CONV_WIDTH, 3 * DELTA_WIDTH), CONV_WIDTH ** -0.5),
        'a_log': jnp.log(jax.random.uniform(ks[8], (DEPTH, N_DELTA_HEADS), f32, minval=1.0, maxval=16.0)),
        'dt_bias': dt + jnp.log(-jnp.expm1(-dt)),
        'delta_norm_g': 1.0 + nrm(ks[10], (DEPTH, HEAD_DIM), 0.05),
        'w_out': nrm(ks[11], (DEPTH, MIX_WIDTH, D_MODEL), MIX_WIDTH ** -0.5),
        'norm_ffn_g': 1.0 + nrm(ks[12], (DEPTH, D_MODEL), 0.05),
        'w_gate': nrm(ks[13], (DEPTH, D_MODEL, D_FF), D_MODEL ** -0.5),
        'w_up': nrm(ks[14], (DEPTH, D_MODEL, D_FF), D_MODEL ** -0.5),
        'w_down': nrm(ks[15], (DEPTH, D_FF, D_MODEL), D_FF ** -0.5),
        'final_norm_g': 1.0 + nrm(ks[16], (D_MODEL,), 0.05),
    }

def second_block(x, c, w_ada, b_ada, norm_attn_g, w_in, rel_bias, conv_w, a_log, dt_bias,
              delta_norm_g, w_out, norm_ffn_g, w_gate, w_up, w_down, final_norm_g):
    bsz, s, _ = x.shape
    split_points = np.cumsum([ATTN_WIDTH] * 3 + [DELTA_WIDTH] * 4 + [N_DELTA_HEADS])
    c_act = jax.nn.silu(c)
    for l in range(DEPTH):
        mod = c_act @ w_ada[l] + b_ada[l]
        sh1, sc1, g1, sh2, sc2, g2 = [m[:, None, :] for m in jnp.split(mod, 6, axis=-1)]
        h = _rmsnorm(x, norm_attn_g[l]) * (1.0 + sc1) + sh1
        proj = h @ w_in[l]
        q_a, k_a, v_a, q_d, k_d, v_d, z_d, b_d, a_d = jnp.split(proj, split_points, axis=-1)
        hs = (bsz, s, N_ATTN_HEADS, HEAD_DIM)
        y_attn = _dilated_attention(q_a.reshape(hs), k_a.reshape(hs), v_a.reshape(hs), rel_bias).astype(x.dtype)
        y_delta = _gated_deltanet(q_d, k_d, v_d, z_d, b_d, a_d, conv_w[l], a_log[l], dt_bias[l], delta_norm_g[l])
        y = jnp.concatenate([y_attn, y_delta], axis=-1) @ w_out[l]
        x = x + g1 * y
        h = _rmsnorm(x, norm_ffn_g[l]) * (1.0 + sc2) + sh2
        y = (jax.nn.silu(h @ w_gate[l]) * (h @ w_up[l])) @ w_down[l]
        x = x + g2 * y
    return _rmsnorm(x, final_norm_g)


def setup_inputs(seed=0):
    out = dict(first_inputs(seed))
    for name, value in second_inputs(seed + 1).items():
        if name != "x":
            out[name + "_2"] = value
    return out


def reference(
    x, c, positions, ada_w, ada_b, norm1_g, norm2_g, w_in, b_fgt, b_gate, qn_fox, kn_fox,
    qn_dsa, kn_dsa, w_proj_fox, w_proj_dsa, w_out, router_w_grp, router_b_grp, router_w_exp,
    router_b_exp, exp_w1, exp_w3, exp_w2, c_2, w_ada_2, b_ada_2, norm_attn_g_2, w_in_2,
    rel_bias_2, conv_w_2, a_log_2, dt_bias_2, delta_norm_g_2, w_out_2, norm_ffn_g_2, w_gate_2,
    w_up_2, w_down_2, final_norm_g_2,
):
    x = first_block(
        x, c, positions, ada_w, ada_b, norm1_g, norm2_g, w_in, b_fgt, b_gate, qn_fox, kn_fox,
        qn_dsa, kn_dsa, w_proj_fox, w_proj_dsa, w_out, router_w_grp, router_b_grp, router_w_exp,
        router_b_exp, exp_w1, exp_w3, exp_w2,
    )
    return second_block(
        x, c_2, w_ada_2, b_ada_2, norm_attn_g_2, w_in_2, rel_bias_2, conv_w_2, a_log_2,
        dt_bias_2, delta_norm_g_2, w_out_2, norm_ffn_g_2, w_gate_2, w_up_2, w_down_2,
        final_norm_g_2,
    )


_drawn_inputs = setup_inputs


def setup_inputs(seed=0):
    import zlib

    import numpy as np

    out = dict(_drawn_inputs(seed))
    spreads = {}
    factors = {'ada_b': 2.975,
     'norm1_g': 5.06,
     'norm2_g': 2.759,
     'b_gate': 8.0,
     'qn_fox': 8.0,
     'kn_fox': 8.0,
     'qn_dsa': 8.0,
     'kn_dsa': 8.0,
     'router_b_grp': 8.0,
     'router_b_exp': 8.0,
     'norm_attn_g_2': 4.325,
     'rel_bias_2': 3.257,
     'delta_norm_g_2': 8.0,
     'norm_ffn_g_2': 3.701}
    for name, (base, spread) in spreads.items():
        noise = np.random.default_rng([zlib.crc32(name.encode()), seed]).standard_normal(out[name].shape)
        drawn = base * np.exp(spread * noise) if base else spread * noise
        out[name] = __import__('jax').numpy.asarray(drawn.astype(out[name].dtype))
    for name, factor in factors.items():
        out[name] = (out[name] * factor).astype(out[name].dtype)
    return out
```

```python
from contextlib import ExitStack, contextmanager

import numpy as np
import concourse.bass as bass
from concourse import mybir

P = 128
S = 1024
D = 1024
NT = S // P
KD = D // P
H = 8
DH = 64
W = H * DH
CH = 512
EPS = 1e-6
NEG = -1e30
FIRST_CHUNKS = 2 * D // CH

C_FQ, C_FK, C_FV, C_FLOG = 0, W, 2 * W, 3 * W
C_DQ = C_FLOG + H
C_DK = C_DQ + W
C_DV = C_DK + DH
C_IQ = C_DV + DH
C_IK = C_IQ + W
C_IW = C_IK + DH
C_GATE = C_IW + H
N1 = C_GATE + 2 * D
C_QA, C_KA, C_VA, C_QKV = 0, W, 2 * W, 3 * W
C_Z = C_QKV + 3 * W
C_B = C_Z + W
C_A = C_B + H
N2 = C_A + H

F32 = mybir.dt.float32
I32 = mybir.dt.int32
U32 = mybir.dt.uint32
ALU = mybir.AluOpType
ACT = mybir.ActivationFunctionType
AX = mybir.AxisListType.X


class Shared:
    pass


class Unit:

    def __init__(self, width, q, mask, k, v):
        self.width, self.q, self.mask, self.k, self.v = width, q, mask, k, v


class Chain:

    def __init__(self, eng, sem):
        self.eng, self.sem, self.count, self.base = eng, sem, 0, 0

    def __call__(self, instruction):
        instruction.then_inc(self.sem, 1)
        self.count += 1
        self.eng.wait_ge(self.sem, self.base + self.count)

    def enter(self, i, per_turn):
        self.entered, self.per_turn = self.count, per_turn
        self.base = i * per_turn

    def leave(self, turns):
        assert self.count == self.entered + self.per_turn, self.count - self.entered
        self.base = 0
        self.count = self.entered + turns * self.per_turn


@contextmanager
def stage(nc, g):
    with ExitStack() as ctx:
        yield ctx
    for sem in g.sems:
        nc.gpsimd.sem_clear(sem)
        nc.release_semaphore(sem)
    g.sems.clear()


def rows(dram):
    return dram.rearrange("(t p) n -> p t n", p=P)


def row_bcast(vec, n):
    return vec.rearrange("(a n) -> a n", a=1).broadcast_to([P, n])


def modulation(nc, g):
    NJ = 6 * D // P
    with stage(nc, g) as ctx:
        sb = lambda name, shape, dt=F32: ctx.enter_context(nc.sbuf_tensor(name, shape, dt))
        pb = lambda name, shape: ctx.enter_context(nc.psum_tensor(name, shape, F32))
        w = [sb(f"ada{b}", [P, KD, CH]) for b in range(2)]
        vec_rows = sb("vec_rows", [6 * KD, P])
        bias_rows = [sb(f"bias_rows{b}", [NJ, P]) for b in range(2)]
        biasT, cT = g.biasT, g.cT
        vec_ps = pb("vec_ps", [P, 512])
        mod_ps = [pb(f"mod_ps{b}", [P, 512]) for b in range(2)]
        small = g.sem("mod_small")
        loaded = [g.sem(f"mod_loaded{b}") for b in range(2)]
        transposed = g.sem("mod_transposed")
        silu = g.sem("mod_silu")
        product = [g.sem(f"mod_product{b}") for b in range(2)]
        taken = [g.sem(f"mod_taken{b}") for b in range(2)]
        smalls = [(g.ident[:, :], g.d["c_ident"]), (bias_rows[0][:, :], g.d["ada_b"][0].rearrange("(r p) -> r p", p=P)),
                  (bias_rows[1][:, :], g.d["b_ada_2"][0].rearrange("(r p) -> r p", p=P))]
        for n, v in enumerate([g.d["c"][0], g.d["c_2"][0], g.d["norm1_g"][0], g.d["norm2_g"][0],
                               g.d["norm_attn_g_2"][0], g.d["norm_ffn_g_2"][0]]):
            smalls.append((vec_rows[n * KD:(n + 1) * KD, :], v.rearrange("(r p) -> r p", p=P)))
        w_dram = g.d["ada_w"][0].rearrange("(k p) n -> p k n", p=P)
        PAIRS = FIRST_CHUNKS // 2
        block = ctx.enter_context(nc.Block())

        @block.sync
        def _(sp):
            for dst, src in smalls:
                sp.dma_start(dst, src).then_inc(small, 16)
            with sp.Fori(0, PAIRS) as i:
                for b in range(2):
                    sp.wait_ge(product[b], i)
                    sp.dma_start(w[b][:, :, :], w_dram[:, :, bass.ds(i * (2 * CH) + b * CH, CH)]).then_inc(loaded[b], 16)

        @block.tensor
        def _(pe):
            pe.wait_ge(small, 16 * len(smalls))
            nc.tensor.transpose(vec_ps[:, 0:48], vec_rows[:, :], g.ident[0:48, 0:48])
            nc.tensor.transpose(vec_ps[:, 48:96], bias_rows[0][:, :], g.ident[0:48, 0:48])
            nc.tensor.transpose(vec_ps[:, 96:144], bias_rows[1][:, :], g.ident[0:48, 0:48]).then_inc(transposed, 1)
            pe.wait_ge(silu, 1)
            with pe.Fori(0, PAIRS) as i:
                for b in range(2):
                    pe.wait_ge(loaded[b], i * 16 + 16)
                    pe.wait_ge(taken[b], i)
                    for j in range(CH // P):
                        for k in range(KD):
                            last = nc.tensor.matmul(mod_ps[b][:, j:j + 1], w[b][:, k, j * P:(j + 1) * P], cT[:, k:k + 1],
                                                    start=k == 0, stop=k == KD - 1)
                    last.then_inc(product[b], 1)

        @block.scalar
        def _(act):
            act.wait_ge(transposed, 1)
            nc.scalar.activation(cT[:, :], vec_ps[:, 0:2 * KD], ACT.Silu).then_inc(silu, 1)

        @block.vector
        def _(dve):
            chain = g.chain(dve)
            nc.vector.memset(g.eps[:, :], EPS)
            dve.wait_ge(silu, 1)
            nc.vector.tensor_copy(g.gainT[:, :], vec_ps[:, 2 * KD:6 * KD])
            chain(nc.vector.tensor_copy(biasT[:, :], vec_ps[:, 48:48 + 2 * NJ]))
            with dve.Fori(0, PAIRS) as i:
                for b in range(2):
                    dve.wait_ge(product[b], i + 1)
                    cols = bass.ds(i * 8 + 4 * b, 4)
                    nc.vector.tensor_tensor(g.modT[:, cols], mod_ps[b][:, 0:4], biasT[:, cols], ALU.add).then_inc(taken[b], 1)


def normalize(nc, g, name, x_dram, blk, half, hT, xn_dram=None):
    with stage(nc, g) as ctx:
        sb = lambda n, shape, dt=F32: ctx.enter_context(nc.sbuf_tensor(name + n, shape, dt))
        x = [sb(f"x{b}", [P, D]) for b in range(2)]
        xn = [sb(f"xn{b}", [P, D]) for b in range(2)]
        square = sb("square", [P, D])
        stat = sb("stat", [P, 2 * NT])
        gain = sb("gain", [P, KD])
        ps = [ctx.enter_context(nc.psum_tensor(f"{name}ps{b}", [P, KD, P], F32)) for b in range(2)]
        loaded = [g.sem(name + f"loaded{b}") for b in range(2)]
        squared = g.sem(name + "squared")
        scaled = g.sem(name + "scaled")
        flipped = g.sem(name + "flipped")
        gain_ready = g.sem(name + "gain_ready")
        done = g.sem(name + "done")
        stored = [g.swdge_sem(name + f"stored{b}") for b in range(2)]
        shift = g.modT[:, 48 * blk + 24 * half:48 * blk + 24 * half + KD]
        scale = g.modT[:, 48 * blk + 24 * half + KD:48 * blk + 24 * half + 2 * KD]
        gains = g.gainT[:, (2 * blk + half) * KD:(2 * blk + half + 1) * KD]
        block = ctx.enter_context(nc.Block())

        @block.sync
        def _(sp):
            for t in range(NT):
                if t >= 2:
                    sp.wait_ge(scaled, t - 1)
                sp.dma_start(x[t % 2][:, :], rows(x_dram)[:, t, :]).then_inc(loaded[t % 2], 16)

        @block.gpsimd
        def _(sp):
            if xn_dram is not None:
                for t in range(NT):
                    sp.wait_ge(scaled, t + 1)
                    sp.dma_start(rows(xn_dram)[:, t, :], xn[t % 2][:, :]).then_inc(stored[t % 2], 16)
                for b in range(2):
                    sp.wait_ge(stored[b], 16 * (NT // 2))

        def write(act, t):
            act.wait_ge(flipped, t + 1)
            if t == 0:
                act.wait_ge(gain_ready, 1)
            for k in range(KD):
                last = nc.scalar.activation(hT[:, k, t * P:(t + 1) * P], ps[t % 2][:, k, :], ACT.Identity,
                                            bias=shift[:, k:k + 1], scale=gain[:, k:k + 1])
            last.then_inc(done, 1)

        @block.scalar
        def _(act):
            chain = g.chain(act)
            for t in range(NT):
                act.wait_ge(loaded[t % 2], 16 * (t // 2 + 1))
                chain(nc.scalar.activation(square[:, :], x[t % 2][:, :], ACT.Square, accum_out=stat[:, t:t + 1]))
                chain(nc.scalar.activation(stat[:, t:t + 1], stat[:, t:t + 1], ACT.Sqrt, scale=1.0 / D, bias=g.eps[:, :]))
                act.sem_inc(squared, 1)
                if t >= 1:
                    write(act, t - 1)
            write(act, NT - 1)

        @block.vector
        def _(dve):
            chain = g.chain(dve)
            chain(nc.vector.tensor_scalar(gain[:, :], scale, 1.0, None, ALU.add))
            nc.vector.tensor_tensor(gain[:, :], gain[:, :], gains, ALU.mult).then_inc(gain_ready, 1)
            for t in range(NT):
                dve.wait_ge(squared, t + 1)
                chain(nc.vector.reciprocal(stat[:, NT + t:NT + t + 1], stat[:, t:t + 1]))
                if t >= 2:
                    dve.wait_ge(flipped, t - 1)
                    if xn_dram is not None:
                        dve.wait_ge(stored[t % 2], 16 * (t // 2))
                nc.vector.tensor_scalar(xn[t % 2][:, :], x[t % 2][:, :], stat[:, NT + t:NT + t + 1], None,
                                        ALU.mult).then_inc(scaled, 1)

        @block.tensor
        def _(pe):
            for t in range(NT):
                pe.wait_ge(scaled, t + 1)
                if t >= 2:
                    pe.wait_ge(done, t - 1)
                for k in range(KD):
                    last = nc.tensor.transpose(ps[t % 2][:, k, :], xn[t % 2][:, k * P:(k + 1) * P], g.ident[:, :])
                last.then_inc(flipped, 1)


def project(nc, g, name, hT, w_dram, cols, out_dram):
    with stage(nc, g) as ctx:
        sb = lambda n, shape, dt=F32: ctx.enter_context(nc.sbuf_tensor(name + n, shape, dt))
        w = [sb(f"w{b}", [P, KD, CH]) for b in range(2)]
        out = [sb(f"out{b}", [P, NT, CH]) for b in range(2)]
        ps = [ctx.enter_context(nc.psum_tensor(f"{name}ps{t}", [P, CH], F32)) for t in range(NT)]
        loaded = [g.sem(name + f"loaded{b}") for b in range(2)]
        product = g.sem(name + "product")
        copied = [g.sem(name + f"copied{e}") for e in range(2)]
        stored = [g.swdge_sem(name + f"stored{b}") for b in range(2)]
        pairs = cols // CH // 2
        rest = [(c, min(CH, cols - c)) for c in range(pairs * 2 * CH, cols, CH)]
        w_v = w_dram.rearrange("(k p) n -> p k n", p=P)
        out_v = rows(out_dram)
        block = ctx.enter_context(nc.Block())

        def load(sp, n_in_buffer, b, col, width):
            sp.dma_start(w[b][:, :, 0:width], w_v[:, :, col]).then_inc(loaded[b], 16)

        @block.sync
        def _(sp):
            with sp.Fori(0, pairs) as i:
                for b in range(2):
                    sp.wait_ge(product, i * (2 * NT) + (b + 1) * NT)
                    load(sp, i, b, bass.ds(i * (2 * CH) + b * CH, CH), CH)
            for n, (c, width) in enumerate(rest):
                sp.wait_ge(product, (2 * pairs + n + 1) * NT)
                load(sp, pairs + n // 2, n % 2, slice(c, c + width), width)

        @block.gpsimd
        def _(pool):
            with pool.Fori(0, pairs) as i:
                for b in range(2):
                    for e in range(2):
                        pool.wait_ge(copied[e], i * NT + (NT // 2) * (b + 2))
                    pool.dma_start(out_v[:, :, bass.ds(i * (2 * CH) + b * CH, CH)], out[b][:, :, :]).then_inc(stored[b], 16)
            for n, (c, width) in enumerate(rest):
                for e in range(2):
                    pool.wait_ge(copied[e], (NT // 2) * (2 * pairs + n + 2))
                pool.dma_start(out_v[:, :, c:c + width], out[n % 2][:, :, 0:width]).then_inc(stored[n % 2], 16)
            for b in range(2):
                pool.wait_ge(stored[b], 16 * (pairs + len(rest[b::2])))

        @block.tensor
        def _(pe):
            pe.sem_inc(product, 2 * NT)

            def chunk(loaded_count, b, width, copied_count):
                pe.wait_ge(loaded[b], loaded_count)
                for t in range(NT):
                    pe.wait_ge(copied[t % 2], copied_count + t // 2 + 1)
                    for k in range(KD):
                        last = nc.tensor.matmul(ps[t][:, 0:width], hT[:, k, t * P:(t + 1) * P], w[b][:, k, 0:width],
                                                start=k == 0, stop=k == KD - 1)
                    last.then_inc(product, 1)
            with pe.Fori(0, pairs) as i:
                for b in range(2):
                    chunk(i * 16 + 16, b, CH, i * NT + b * (NT // 2))
            for n, (c, width) in enumerate(rest):
                chunk(16 * (pairs + n // 2 + 1), n % 2, width, (NT // 2) * (2 * pairs + n))

        def copies(eng, e, copy):
            eng.sem_inc(copied[e], NT // 2)

            def chunk(product_count, b, width, stored_count):
                eng.wait_ge(stored[b], stored_count)
                for t in range(e, NT, 2):
                    eng.wait_ge(product, product_count + t + 1)
                    copy(out[b][:, t, 0:width], ps[t][:, 0:width]).then_inc(copied[e], 1)
            with eng.Fori(0, pairs) as i:
                for b in range(2):
                    chunk(i * (2 * NT) + (b + 2) * NT, b, CH, i * 16)
            for n, (c, width) in enumerate(rest):
                chunk((2 * pairs + n + 2) * NT, n % 2, width, 16 * (pairs + n // 2))

        @block.vector
        def _(dve):
            copies(dve, 0, nc.vector.tensor_copy)

        @block.scalar
        def _(act):
            copies(act, 1, nc.scalar.copy)


def shared(nc, ctx, dram):
    sb = lambda name, shape: ctx.enter_context(nc.sbuf_tensor(name, shape, F32))
    g = Shared()
    g.d = dram
    g.sems = []

    def sem(name):
        g.sems.append(nc.alloc_semaphore(name))
        return g.sems[-1]
    g.sem = sem
    g.swdge_sem = nc.alloc_semaphore
    g.ident = sb("ident", [P, P])
    g.eps = sb("eps", [P, 1])
    g.biasT, g.cT = sb("biasT", [P, 96]), sb("cT", [P, 2 * KD])
    g.experts = ctx.enter_context(nc.sbuf_tensor("experts", [1, 64], I32))
    g.modT = sb("modT", [P, 96])
    g.gainT = sb("gainT", [P, 32])
    g.chain = lambda eng: Chain(eng, g.sem(f"chain{nc.next_id()}"))
    return g


def attention(nc, g, name, units, out_width, raw, store, loads=()):
    with stage(nc, g) as ctx:
        sb = lambda n, shape, dt=F32: ctx.enter_context(nc.sbuf_tensor(name + n, shape, dt))
        widest = max(u.width for u in units)
        e = [sb(f"e{b}", [P, widest]) for b in range(2)]
        eT = [sb(f"eT{b}", [P, widest // P, P]) for b in range(2)]
        out = [sb(f"out{b}", [P, H, out_width]) for b in range(2)]
        nmax = sb("nmax", [P, 2])
        total = sb("total", [P, 4])
        rtotal = sb("rtotal", [P, 2])
        s_ps = [ctx.enter_context(nc.psum_tensor(f"{name}s{b}", [P, 2, CH], F32)) for b in range(2)]
        t_ps = [ctx.enter_context(nc.psum_tensor(f"{name}t{b}", [P, 4, P], F32)) for b in range(2)]
        o_ps = [ctx.enter_context(nc.psum_tensor(f"{name}o{b}", [P, CH], F32)) for b in range(2)]
        loaded = g.sem(name + "loaded")
        scored = g.sem(name + "scored")
        maxed = g.sem(name + "maxed")
        exped = g.sem(name + "exped")
        flipped = g.sem(name + "flipped")
        copied = [g.sem(name + f"copied{p}") for p in range(2)]
        weighted = g.sem(name + "weighted")
        taken = g.sem(name + "taken")
        stored = [g.sem(name + f"stored{b}") for b in range(2)]
        U = len(units)
        stores = lambda run, b: sum(16 * len(store(n)) for n in range(b, run, 2))
        groups, first = [], 0
        for u in units:
            tiles = list(range(u.width // P))
            groups.append([(first + n, tiles[4 * n:4 * n + 4]) for n in range((len(tiles) + 3) // 4)])
            first += len(groups[-1])
        group_end = [gr[-1][0] + 1 for gr in groups]
        flat = lambda t, w: t[:, :, :].rearrange("p a b -> p (a b)")[:, 0:w]
        block = ctx.enter_context(nc.Block())

        @block.sync
        def _(sp):
            for dst, src in loads:
                sp.dma_start(dst, src).then_inc(loaded, 16)
            for n in range(U // H):
                sp.wait_ge(taken, H * (n + 1))
                for dst, p0, p1 in store(n):
                    sp.dma_start(dst, out[n % 2][p0:p1, :, :]).then_inc(stored[n % 2], 16)
            for b in range(2):
                sp.wait_ge(stored[b], stores(U // H, b))

        @block.tensor
        def _(pe):
            def scores(u):
                if u >= 2:
                    pe.wait_ge(exped, u - 1)
                for c in range(0, units[u].width, CH):
                    w = min(CH, units[u].width - c)
                    last = nc.tensor.matmul(s_ps[u % 2][:, c // CH, 0:w], units[u].q, units[u].k(c, w), start=True, stop=True)
                last.then_inc(scored, 1)

            def values(u):
                pe.wait_ge(copied[0], (group_end[u] + 1) // 2)
                if group_end[u] // 2:
                    pe.wait_ge(copied[1], group_end[u] // 2)
                if u >= 2:
                    pe.wait_ge(taken, u - 1)
                n = units[u].width // P
                for j in range(n):
                    last = nc.tensor.matmul(o_ps[u % 2][:, 0:DH], eT[u % 2][:, j, :], units[u].v(j), start=j == 0, stop=j == n - 1)
                last.then_inc(weighted, 1)

            if loads:
                pe.wait_ge(loaded, 16 * len(loads))
            scores(0)
            for u in range(U):
                if u + 1 < U:
                    scores(u + 1)
                pe.wait_ge(exped, u + 1)
                for n, tiles in groups[u]:
                    if n >= 2:
                        pe.wait_ge(copied[n % 2], n // 2)
                    for j in tiles:
                        last = nc.tensor.transpose(t_ps[n % 2][:, j % 4, :], e[u % 2][:, j * P:(j + 1) * P], g.ident[:, :])
                    last.then_inc(flipped, 1)
                if u >= 1:
                    values(u - 1)
            values(U - 1)

        def copies(eng, u, parity, copy):
            for n, tiles in groups[u]:
                if n % 2 == parity:
                    eng.wait_ge(flipped, n + 1)
                    if u >= 2:
                        eng.wait_ge(weighted, u - 1)
                    copy(eT[u % 2][:, tiles[0]:tiles[-1] + 1, :], t_ps[parity][:, 0:len(tiles), :]).then_inc(copied[parity], 1)

        @block.vector
        def _(dve):
            chain = g.chain(dve)
            if loads:
                dve.wait_ge(loaded, 16 * len(loads))

            def maximum(u):
                dve.wait_ge(scored, u + 1)
                mask, c0 = units[u].mask
                w = units[u].width
                for c in range(0, w, CH):
                    lo, hi = max(c, c0), min(c + CH, w)
                    if lo < hi:
                        part = s_ps[u % 2][:, c // CH, lo - c:hi - c]
                        last = nc.vector.tensor_tensor(part, part, mask[:, lo - c0:hi - c0], ALU.add)
                chain(last)
                if u >= 2:
                    dve.wait_ge(exped, u - 1)
                nc.vector.tensor_reduce(nmax[:, u % 2:u % 2 + 1], flat(s_ps[u % 2], w), AX, ALU.max, negate=True).then_inc(maxed, 1)

            def result(u):
                run, head = u // H, u % H
                dve.wait_ge(weighted, u + 1)
                if run >= 2 and head == 0:
                    dve.wait_ge(stored[run % 2], stores(run, run % 2))
                o = out[run % 2]
                if raw:
                    nc.vector.tensor_copy(o[:, head, 64:65], keep[:, u % 4:u % 4 + 1])
                    nc.vector.tensor_copy(o[:, head, 65:66], total[:, u % 4:u % 4 + 1])
                    nc.vector.tensor_copy(o[:, head, 0:DH], o_ps[u % 2][:, 0:DH]).then_inc(taken, 1)
                else:
                    chain(nc.vector.reciprocal(rtotal[:, u % 2:u % 2 + 1], total[:, u % 4:u % 4 + 1]))
                    nc.vector.tensor_scalar(o[:, head, :], o_ps[u % 2][:, 0:DH], rtotal[:, u % 2:u % 2 + 1], None, ALU.mult).then_inc(taken, 1)

            if raw:
                keep = sb("keep", [P, 4])
            for u in range(-1, U + 1):
                if u + 1 < U:
                    maximum(u + 1)
                    if raw:
                        dve.wait_ge(maxed, u + 2)
                        nc.vector.tensor_copy(keep[:, (u + 1) % 4:(u + 1) % 4 + 1], nmax[:, (u + 1) % 2:(u + 1) % 2 + 1])
                if 0 <= u < U:
                    copies(dve, u, 0, nc.vector.tensor_copy)
                if u >= 1:
                    result(u - 1)

        @block.scalar
        def _(act):
            for u in range(-1, U):
                if u + 1 < U:
                    n = u + 1
                    act.wait_ge(maxed, n + 1)
                    if n >= 2:
                        act.wait_ge(flipped, group_end[n - 2])
                    if n >= 4:
                        act.wait_ge(taken, n - 3)
                    w = units[n].width
                    nc.scalar.activation(e[n % 2][:, 0:w], flat(s_ps[n % 2], w), ACT.Exp,
                                         bias=nmax[:, n % 2:n % 2 + 1], accum_out=total[:, n % 4:n % 4 + 1]).then_inc(exped, 1)
                if u >= 0:
                    copies(act, u, 1, nc.scalar.copy)


def fox_prepare(nc, g, qT, kT):
    A = DH + 2
    with stage(nc, g) as ctx:
        sb = lambda n, shape, dt=F32: ctx.enter_context(nc.sbuf_tensor("fp_" + n, shape, dt))
        x = [sb(f"x{b}", [P, 2 * W]) for b in range(2)]
        aug = [sb(f"aug{b}", [P, 2 * H, A]) for b in range(2)]
        square = sb("square", [P, 2 * H, DH])
        stat = sb("stat", [P, 2 * H])
        gain = sb("gain", [P, 2 * H, DH])
        lf = sb("lf", [P, NT, H])
        tmp = sb("tmp", [P, NT, H])
        bias = sb("bias", [P, H])
        total = sb("total", [P, NT, H])
        F = sb("F", [P, NT, H])
        tri = sb("tri", [P, P])
        ones = sb("ones", [P, P])
        c_ps = ctx.enter_context(nc.psum_tensor("fp_c", [P, CH], F32))
        o_ps = ctx.enter_context(nc.psum_tensor("fp_o", [P, CH], F32))
        t_ps = [ctx.enter_context(nc.psum_tensor(f"fp_t{b}", [A, 4, P], F32)) for b in range(4)]
        small = g.sem("fp_small")
        loaded = [g.sem(f"fp_loaded{b}") for b in range(2)]
        logf = g.sem("fp_logf")
        summed = g.sem("fp_summed")
        tot = g.sem("fp_tot")
        squared = g.sem("fp_squared")
        rooted = g.sem("fp_rooted")
        ready = g.sem("fp_ready")
        flipped = g.sem("fp_flipped")
        copied = g.sem("fp_copied")
        block = ctx.enter_context(nc.Block())
        qn, kn = row_bcast(g.d["qn_fox"][0], DH), row_bcast(g.d["kn_fox"][0], DH)
        smalls = [(tri[:, :], g.d["c_tri"]), (lf[:, :, :], rows(g.d["proj1"])[:, :, C_FLOG:C_FLOG + H]),
                  (bias[:, :], row_bcast(g.d["b_fgt"][0], H))]
        smalls += [(gain[:, h, :], qn if h < H else kn) for h in range(2 * H)]

        @block.sync
        def _(sp):
            for dst, src in smalls:
                sp.dma_start(dst, src).then_inc(small, 16)
            for t in range(NT):
                if t >= 2:
                    sp.wait_ge(ready, t - 1)
                sp.dma_start(x[t % 2][:, :], rows(g.d["proj1"])[:, t, C_FQ:C_FQ + 2 * W]).then_inc(loaded[t % 2], 16)

        @block.scalar
        def _(act):
            chain = g.chain(act)
            act.wait_ge(logf, 1)
            chain(nc.scalar.activation(tmp[:, :, :], lf[:, :, :], ACT.Abs))
            chain(nc.scalar.activation(tmp[:, :, :], tmp[:, :, :], ACT.Exp, scale=-1.0))
            nc.scalar.activation(tmp[:, :, :], tmp[:, :, :], ACT.Ln, bias=1.0).then_inc(logf, 1)
            for t in range(NT):
                act.wait_ge(squared, t + 1)
                nc.scalar.activation(stat[:, :], stat[:, :], ACT.Sqrt, scale=1.0 / DH, bias=g.eps[:, :]).then_inc(rooted, 1)
                for n in range(4 * t, 4 * t + 4):
                    act.wait_ge(flipped, n + 1)
                    to = qT if n % 4 < 2 else kT
                    h = 4 * (n % 2)
                    nc.scalar.copy(to[:, h:h + 4, t * P:(t + 1) * P], t_ps[n % 4][:, :, :]).then_inc(copied, 1)

        @block.vector
        def _(dve):
            chain = g.chain(dve)
            bc = lambda ap: ap.unsqueeze(1).broadcast_to([P, NT, H])
            nc.vector.memset(ones[:, :], 1.0)
            dve.wait_ge(small, 16 * len(smalls))
            chain(nc.vector.tensor_scalar(gain[:, 0:H, :], gain[:, 0:H, :], DH ** -0.5, None, ALU.mult))
            nc.vector.tensor_tensor(lf[:, :, :], lf[:, :, :], bc(bias[:, :]), ALU.add).then_inc(logf, 1)
            dve.wait_ge(logf, 2)
            chain(nc.vector.tensor_scalar(lf[:, :, :], lf[:, :, :], 0.0, None, ALU.min))
            nc.vector.tensor_tensor(lf[:, :, :], lf[:, :, :], tmp[:, :, :], ALU.subtract).then_inc(summed, 1)
            dve.wait_ge(tot, 1)
            chain(nc.vector.memset(total[:, 0, :], 0.0))
            for t in range(1, NT):
                chain(nc.vector.tensor_tensor(total[:, t, :], total[:, t - 1, :], o_ps[:, (t - 1) * H:t * H], ALU.add))
            chain(nc.vector.tensor_tensor(F[:, :, :].rearrange("p a b -> p (a b)"), c_ps[:, 0:NT * H],
                                          total[:, :, :].rearrange("p a b -> p (a b)"), ALU.add))
            for b in range(2):
                nc.vector.memset(aug[b][:, 0:H, DH + 1:A], 1.0)
                nc.vector.memset(aug[b][:, H:2 * H, DH:DH + 1], 1.0)
            for t in range(NT):
                dve.wait_ge(loaded[t % 2], 16 * (t // 2 + 1))
                xv = x[t % 2][:, :].rearrange("p (h d) -> p h d", d=DH)
                if t >= 1:
                    dve.wait_ge(ready, t)
                chain(nc.vector.tensor_tensor(square[:, :, :], xv, xv, ALU.mult))
                nc.vector.tensor_reduce(stat[:, :], square[:, :, :], AX, ALU.add).then_inc(squared, 1)
                if t >= 2:
                    dve.wait_ge(flipped, 4 * (t - 1))
                nc.vector.tensor_copy(aug[t % 2][:, 0:H, DH:DH + 1], F[:, t, :].unsqueeze(2))
                nc.vector.tensor_scalar(aug[t % 2][:, H:2 * H, DH + 1:A], F[:, t, :].unsqueeze(2), -1.0, None, ALU.mult)
                dve.wait_ge(rooted, t + 1)
                chain(nc.vector.reciprocal(stat[:, :], stat[:, :]))
                chain(nc.vector.tensor_tensor(square[:, :, :], xv, stat[:, :].unsqueeze(2).broadcast_to([P, 2 * H, DH]), ALU.mult))
                nc.vector.tensor_tensor(aug[t % 2][:, :, 0:DH], square[:, :, :], gain[:, :, :], ALU.mult).then_inc(ready, 1)

        @block.tensor
        def _(pe):
            pe.wait_ge(summed, 1)
            v = lf[:, :, :].rearrange("p a b -> p (a b)")
            nc.tensor.matmul(c_ps[:, 0:NT * H], tri[:, :], v, start=True, stop=True)
            nc.tensor.matmul(o_ps[:, 0:NT * H], ones[:, :], v, start=True, stop=True).then_inc(tot, 1)
            for t in range(NT):
                pe.wait_ge(ready, t + 1)
                for n in range(4 * t, 4 * t + 4):
                    if n >= 4:
                        pe.wait_ge(copied, n - 3)
                    for j in range(4):
                        last = nc.tensor.transpose(t_ps[n % 4][:, j, :], aug[t % 2][:, 4 * (n % 4) + j, :], g.ident[:, :])
                    last.then_inc(flipped, 1)


def forgetting(nc, g):
    with ExitStack() as ctx:
        sb = lambda n, shape: ctx.enter_context(nc.sbuf_tensor("fox_" + n, shape, F32))
        qT, kT = sb("qT", [DH + 2, H, S]), sb("kT", [DH + 2, H, S])
        v, causal = sb("v", [P, NT, W]), sb("causal", [P, P])
        fox_prepare(nc, g, qT, kT)
        units = []
        for t in range(NT):
            for h in range(H):
                units.append(Unit(
                    width=(t + 1) * P, q=qT[:, h, t * P:(t + 1) * P], mask=(causal[:, :], t * P),
                    k=lambda c, w, h=h: kT[:, h, c:c + w], v=lambda j, h=h: v[:, j, h * DH:(h + 1) * DH]))
        attention(nc, g, "fox", units, DH, False, lambda t: [(rows(g.d["out_fox"])[:, t, :].rearrange("p (h d) -> p h d", d=DH), 0, P)],
                  [(v[:, :, :], rows(g.d["proj1"])[:, :, C_FV:C_FV + W]), (causal[:, :], g.d["c_causal"])])


def sparse_prepare(nc, g, dqT, dkT, iqT, ikT):
    G = H + 1
    HF = DH // 2
    with stage(nc, g) as ctx:
        sb = lambda n, shape, dt=F32: ctx.enter_context(nc.sbuf_tensor("sp_" + n, shape, dt))
        x = [sb(f"x{b}", [P, 2, G, DH]) for b in range(2)]
        y = [sb(f"y{b}", [P, 2, G, DH]) for b in range(2)]
        square = sb("square", [P, G, DH])
        part = sb("part", [P, 2, G, HF])
        stat = sb("stat", [P, G])
        gain = sb("gain", [P, G, DH])
        pos_i = sb("pos_i", [P, NT, 1], I32)
        pos = sb("pos", [P, NT])
        inv = sb("inv", [P, HF])
        ang = sb("ang", [P, NT, HF])
        turn = sb("turn", [P, NT, HF])
        sin = sb("sin", [P, NT, HF])
        cos = sb("cos", [P, NT, HF])
        t_ps = [ctx.enter_context(nc.psum_tensor(f"sp_t{b}", [DH, 4, P], F32)) for b in range(5)]
        small = g.sem("sp_small")
        loaded = [g.sem(f"sp_loaded{b}") for b in range(2)]
        angle = g.sem("sp_angle")
        squared = g.sem("sp_squared")
        rooted = g.sem("sp_rooted")
        ready = g.sem("sp_ready")
        flipped = g.sem("sp_flipped")
        copied = g.sem("sp_copied")
        smalls = [(pos_i[:, :, :], g.d["positions"][0].rearrange("(t p u) -> p t u", p=P, u=1)), (inv[:, :], row_bcast(g.d["c_inv"], HF))]
        smalls += [(gain[:, h, :], row_bcast((g.d["qn_dsa"] if h < H else g.d["kn_dsa"])[0], DH)) for h in range(G)]
        jobs = [(0, 0, 4, dqT), (0, 4, 8, dqT), (1, 0, 4, iqT), (1, 4, 8, iqT), (None, 0, 2, None)]
        block = ctx.enter_context(nc.Block())

        @block.sync
        def _(sp):
            for dst, src in smalls:
                sp.dma_start(dst, src, allow_slow_non_contiguous=dst.dtype == I32).then_inc(small, 16)
            for t in range(NT):
                if t >= 2:
                    sp.wait_ge(ready, t - 1)
                for s, c in enumerate((C_DQ, C_IQ)):
                    sp.dma_start(x[t % 2][:, s, :, :], rows(g.d["proj1"])[:, t, c:c + G * DH].rearrange("p (h d) -> p h d", d=DH)).then_inc(loaded[t % 2], 16)

        @block.scalar
        def _(act):
            act.wait_ge(angle, 1)
            nc.scalar.activation(sin[:, :, :], sin[:, :, :], ACT.Sin)
            nc.scalar.activation(cos[:, :, :], cos[:, :, :], ACT.Sin).then_inc(angle, 1)
            for t in range(NT):
                act.wait_ge(squared, t + 1)
                nc.scalar.activation(stat[:, :], stat[:, :], ACT.Sqrt, scale=1.0 / DH, bias=g.eps[:, :]).then_inc(rooted, 1)
                cols = slice(t * P, (t + 1) * P)
                for n, (s, h0, h1, to) in enumerate(jobs):
                    act.wait_ge(flipped, 5 * t + n + 1)
                    if to is not None:
                        nc.scalar.copy(to[:, h0:h1, cols], t_ps[n][:, :, :]).then_inc(copied, 1)
                    else:
                        nc.scalar.copy(dkT[:, cols], t_ps[n][:, 0, :])
                        nc.scalar.copy(ikT[:, cols], t_ps[n][:, 1, :]).then_inc(copied, 1)

        @block.tensor
        def _(pe):
            for t in range(NT):
                pe.wait_ge(ready, t + 1)
                for n, (s, h0, h1, to) in enumerate(jobs):
                    if t >= 1:
                        pe.wait_ge(copied, 5 * (t - 1) + n + 1)
                    for j in range(h0, h1):
                        src = y[t % 2][:, s, j, :] if to is not None else y[t % 2][:, j, H, :]
                        last = nc.tensor.transpose(t_ps[n][:, j - h0, :], src, g.ident[:, :])
                    last.then_inc(flipped, 1)

        @block.vector
        def _(dve):
            chain = g.chain(dve)
            T = nc.vector.tensor_tensor
            dve.wait_ge(small, 16 * len(smalls))
            chain(nc.vector.tensor_copy(pos[:, :], pos_i[:, :, 0]))
            chain(nc.vector.tensor_scalar(gain[:, 0:H, :], gain[:, 0:H, :], DH ** -0.5, None, ALU.mult))
            chain(T(ang[:, :, :], pos[:, :].unsqueeze(2).broadcast_to([P, NT, HF]), inv[:, :].unsqueeze(1).broadcast_to([P, NT, HF]), ALU.mult))
            ROUND = 1.5 * 2.0 ** 23
            c1 = 6.28125
            c2 = float(np.float32(np.round((2 * np.pi - c1) * 2 ** 21) / 2 ** 21))
            c3 = float(np.float32(2 * np.pi - c1 - c2))
            chain(nc.vector.tensor_scalar(turn[:, :, :], ang[:, :, :], float(1 / (2 * np.pi)), None, ALU.mult))
            chain(nc.vector.tensor_scalar(turn[:, :, :], turn[:, :, :], ROUND, None, ALU.add))
            chain(nc.vector.tensor_scalar(turn[:, :, :], turn[:, :, :], ROUND, None, ALU.subtract))
            for c in (c1, c2, c3):
                chain(nc.vector.scalar_tensor_tensor(ang[:, :, :], turn[:, :, :], -c, ang[:, :, :], ALU.mult, ALU.add))
            lim = 3.1415925
            chain(nc.vector.tensor_scalar(sin[:, :, :], ang[:, :, :], lim, -lim, ALU.min, ALU.max))
            chain(nc.vector.tensor_scalar(turn[:, :, :], ang[:, :, :], -1.0, None, ALU.mult))
            chain(T(ang[:, :, :], ang[:, :, :], turn[:, :, :], ALU.max))
            nc.vector.tensor_scalar(cos[:, :, :], ang[:, :, :], -1.0, float(np.pi / 2), ALU.mult, ALU.add).then_inc(angle, 1)
            dve.wait_ge(angle, 2)
            for t in range(NT):
                dve.wait_ge(loaded[t % 2], 32 * (t // 2 + 1))
                if t >= 1:
                    dve.wait_ge(ready, t)
                X, Y = x[t % 2], y[t % 2]
                chain(T(square[:, :, :], X[:, 0, :, :], X[:, 0, :, :], ALU.mult))
                nc.vector.tensor_reduce(stat[:, :], square[:, :, :], AX, ALU.add).then_inc(squared, 1)
                dve.wait_ge(rooted, t + 1)
                chain(nc.vector.reciprocal(stat[:, :], stat[:, :]))
                chain(T(square[:, :, :], X[:, 0, :, :], stat[:, :].unsqueeze(2).broadcast_to([P, G, DH]), ALU.mult))
                chain(T(X[:, 0, :, :], square[:, :, :], gain[:, :, :], ALU.mult))
                if t >= 2:
                    dve.wait_ge(flipped, 5 * (t - 1))
                for s in range(2):
                    cb = cos[:, t, :].unsqueeze(1).broadcast_to([P, G, HF])
                    sn = sin[:, t, :].unsqueeze(1).broadcast_to([P, G, HF])
                    a, b = X[:, s, :, 0:HF], X[:, s, :, HF:DH]
                    chain(T(part[:, 0, :, :], b, sn, ALU.mult))
                    chain(T(part[:, 1, :, :], a, sn, ALU.mult))
                    T(Y[:, s, :, 0:HF], a, cb, ALU.mult)
                    chain(T(Y[:, s, :, HF:DH], b, cb, ALU.mult))
                    chain(T(Y[:, s, :, 0:HF], Y[:, s, :, 0:HF], part[:, 0, :, :], ALU.subtract))
                    last = T(Y[:, s, :, HF:DH], Y[:, s, :, HF:DH], part[:, 1, :, :], ALU.add)
                    if s == 0:
                        chain(last)
                    else:
                        last.then_inc(ready, 1)


TOPK = 256
CHOSEN = -3e38
HIDDEN = -1e38


def mask_offset(t):
    return P * t * (t + 1) // 2


def side_work():
    ada = [(0, c) for c in range(FIRST_CHUNKS * CH, 6 * D, CH)] + [(1, c) for c in range(0, 6 * D, CH)]
    gates = [(2, c) for c in range(C_GATE, N1, CH)]
    chunks = []
    for n, a in enumerate(ada):
        if n % 5 == 2:
            chunks.append(gates.pop(0))
        chunks.append(a)
    chunks += gates
    tasks = []
    for n, (m, c) in enumerate(chunks):
        tasks += [(n, t) for t in range(NT)] if m == 2 else [(n, None)]
    cost = lambda task: 9.0 if task[1] is None else 6.9
    first = TOPK // P
    ends = np.cumsum([t + 1.0 for t in range(first, NT)])
    whole, done, shares = sum(map(cost, tasks)), 0.0, [[] for _ in ends]
    for task in tasks:
        shares[int(np.searchsorted(ends / ends[-1], done / whole, side="right"))].append(task)
        done += cost(task)
    return chunks, shares


def choose(nc, g, iqT, ikT, mask, hT):
    with stage(nc, g) as ctx:
        sb = lambda n, shape, dt=F32: ctx.enter_context(nc.sbuf_tensor("ch_" + n, shape, dt))
        relu = [sb(f"relu{b}", [P, S]) for b in range(2)]
        score = [sb(f"score{b}", [P, S]) for b in range(2)]
        best = sb("best", [P, 8])
        wi = sb("wi", [P, NT, H])
        s_ps = [ctx.enter_context(nc.psum_tensor(f"ch_s{b}", [P, 2, CH], F32)) for b in range(2)]
        w = [sb(f"w{b}", [P, KD, CH]) for b in range(2)]
        gate = [sb(f"gate{b}", [P, CH]) for b in range(2)]
        side_ps = [ctx.enter_context(nc.psum_tensor(f"ch_side{b}", [P, CH], F32)) for b in range(2)]
        loaded, dots = g.sem("ch_loaded"), g.sem("ch_dots")
        rectified, used = g.sem("ch_rectified"), g.sem("ch_used")
        w_loaded = [g.sem(f"ch_w_loaded{b}") for b in range(2)]
        chunk_used, side_done, side_copied = g.sem("ch_chunk_used"), g.sem("ch_side_done"), g.sem("ch_side_copied")
        gate_stored = [g.sem(f"ch_gate_stored{b}") for b in range(2)]
        biased = g.sem("ch_biased")
        first = TOPK // P
        units = [(t, h) for t in range(first, NT) for h in range(H)]
        chunks, shares = side_work()
        tasks = [task for share in shares for task in share]
        matrices = [m.rearrange("(k p) n -> p k n", p=P) for m in (g.d["ada_w"][0], g.d["w_ada_2"][0], g.d["w_in"][0])]
        flat = lambda t, w: t[:, :, :].rearrange("p a b -> p (a b)")[:, 0:w]
        block = ctx.enter_context(nc.Block())

        @block.sync
        def _(sp):
            sp.dma_start(wi[:, :, :], rows(g.d["proj1"])[:, :, C_IW:C_IW + H]).then_inc(loaded, 16)
            for n, (m, c) in enumerate(chunks):
                if n >= 2:
                    sp.wait_ge(chunk_used, n - 1)
                sp.dma_start(w[n % 2][:, :, :], matrices[m][:, :, c:c + CH]).then_inc(w_loaded[n % 2], 16)

        @block.tensor
        def _(pe):
            def side(i, n, t):
                m, c = chunks[n]
                pe.wait_ge(w_loaded[n % 2], 16 * (n // 2 + 1))
                if i >= 2:
                    pe.wait_ge(side_copied, i - 1)
                if m == 2:
                    for k in range(KD):
                        last = nc.tensor.matmul(side_ps[i % 2][:, :], hT[:, k, t * P:(t + 1) * P], w[n % 2][:, k, :], start=k == 0, stop=k == KD - 1)
                else:
                    for j in range(CH // P):
                        for k in range(KD):
                            last = nc.tensor.matmul(side_ps[i % 2][:, j:j + 1], w[n % 2][:, k, j * P:(j + 1) * P],
                                                    g.cT[:, m * KD + k:m * KD + k + 1], start=k == 0, stop=k == KD - 1)
                last.then_inc(side_done, 1)
                if t in (None, NT - 1):
                    pe.wait_ge(side_done, i + 1)
                    pe.sem_inc(chunk_used, 1)

            i = 0
            for u, (t, h) in enumerate(units):
                if u >= 2:
                    pe.wait_ge(rectified, u - 1)
                w_ = (t + 1) * P
                for c in range(0, w_, CH):
                    n = min(CH, w_ - c)
                    last = nc.tensor.matmul(s_ps[u % 2][:, c // CH, 0:n], iqT[:, h, t * P:(t + 1) * P], ikT[:, c:c + n], start=True, stop=True)
                last.then_inc(dots, 1)
                if h == H - 1:
                    for n, row in shares[t - first]:
                        side(i, n, row)
                        i += 1

        @block.scalar
        def _(act):
            def side(i, n, t):
                m, c = chunks[n]
                act.wait_ge(side_done, i + 1)
                if m == 2:
                    k = gates_before[i]
                    if k >= 2:
                        act.wait_ge(gate_stored[k % 2], 16 * (k // 2))
                    nc.scalar.copy(gate[k % 2][:, :], side_ps[i % 2][:, :]).then_inc(side_copied, 1)
                    act.wait_ge(side_copied, i + 1)
                    act.dma_start(rows(g.d["proj1"])[:, t, c:c + CH], gate[k % 2][:, :]).then_inc(gate_stored[k % 2], 16)
                else:
                    nc.scalar.copy(g.modT[:, 48 * m + c // P:48 * m + c // P + CH // P], side_ps[i % 2][:, 0:CH // P]).then_inc(side_copied, 1)

            gates_before = [sum(t is not None for _, t in tasks[:i]) for i in range(len(tasks) + 1)]
            i = 0
            for u, (t, h) in enumerate(units):
                act.wait_ge(dots, u + 1)
                if u >= 2:
                    act.wait_ge(used, u - 1)
                w_ = (t + 1) * P
                nc.scalar.activation(relu[u % 2][:, 0:w_], flat(s_ps[u % 2], w_), ACT.Relu).then_inc(rectified, 1)
                if h == H - 1:
                    for n, row in shares[t - first]:
                        side(i, n, row)
                        i += 1
            for b in range(2):
                act.wait_ge(gate_stored[b], 16 * ((gates_before[-1] + 1 - b) // 2))

        @block.gpsimd
        def _(pool):
            pool.wait_ge(side_copied, len(tasks))
            cols = slice(FIRST_CHUNKS * CH // P, 96)
            nc.gpsimd.tensor_tensor(g.modT[:, cols], g.modT[:, cols], g.biasT[:, cols], ALU.add).then_inc(biased, 1)

        @block.vector
        def _(dve):
            chain = g.chain(dve)
            dve.wait_ge(loaded, 16)
            u = 0
            for t in range(NT):
                w = (t + 1) * P
                m = mask[:, mask_offset(t):mask_offset(t) + w]
                if t < first:
                    chain(nc.vector.memset(m, 0.0))
                    chain(nc.vector.memset(m[0:DH, w - DH:w], NEG))
                    continue
                sc = score[t % 2][:, 0:w]
                for h in range(H):
                    dve.wait_ge(rectified, u + 1)
                    if h >= 1:
                        dve.wait_ge(used, u)
                    if h == 0:
                        nc.vector.tensor_scalar(sc, relu[u % 2][:, 0:w], wi[:, t, h:h + 1], None, ALU.mult).then_inc(used, 1)
                    else:
                        nc.vector.scalar_tensor_tensor(sc, relu[u % 2][:, 0:w], wi[:, t, h:h + 1], sc, ALU.mult, ALU.add).then_inc(used, 1)
                    u += 1
                dve.wait_ge(used, u)
                chain(nc.vector.memset(sc[0:DH, w - DH:w], HIDDEN))
                for n in range(TOPK // 8):
                    chain(nc.vector.max(best[:, :], sc))
                    chain(nc.vector.match_replace(sc, best[:, :], sc, CHOSEN))
                chain(nc.vector.tensor_scalar(m, sc, (CHOSEN + HIDDEN) / 2, NEG, ALU.is_gt, ALU.mult))


def sparse(nc, g, hT):
    with ExitStack() as ctx:
        sb = lambda n, shape: ctx.enter_context(nc.sbuf_tensor("dsa_" + n, shape, F32))
        dqT, dkT = sb("dqT", [DH, H, S]), sb("dkT", [DH, S])
        mask = sb("mask", [P, mask_offset(NT)])
        with ExitStack() as inner:
            iqT = inner.enter_context(nc.sbuf_tensor("dsa_iqT", [DH, H, S], F32))
            ikT = inner.enter_context(nc.sbuf_tensor("dsa_ikT", [DH, S], F32))
            sparse_prepare(nc, g, dqT, dkT, iqT, ikT)
            choose(nc, g, iqT, ikT, mask, hT)
        v = sb("v", [P, NT, DH])
        units = []
        for t in range(NT):
            for h in range(H):
                units.append(Unit(
                    width=(t + 1) * P, q=dqT[:, h, t * P:(t + 1) * P],
                    mask=(mask[:, mask_offset(t):mask_offset(t + 1)], 0),
                    k=lambda c, w: dkT[:, c:c + w], v=lambda j: v[:, j, :]))
        attention(nc, g, "dsa", units, DH, False, lambda t: [(rows(g.d["out_dsa"])[:, t, :].rearrange("p (h d) -> p h d", d=DH), 0, P)],
                  [(v[:, :, :], rows(g.d["proj1"])[:, :, C_DV:C_DV + DH])])


def transpose_rows(nc, g, name, sources, T):
    K = T.shape[1]
    with stage(nc, g) as ctx:
        x = [ctx.enter_context(nc.sbuf_tensor(f"{name}x{b}", [P, K * P], F32)) for b in range(2)]
        ps = [ctx.enter_context(nc.psum_tensor(f"{name}ps{b}", [P, K, P], F32)) for b in range(2)]
        loaded = [g.sem(name + f"loaded{b}") for b in range(2)]
        flipped, copied = g.sem(name + "flipped"), g.sem(name + "copied")
        block = ctx.enter_context(nc.Block())

        @block.sync
        def _(sp):
            for t in range(NT):
                if t >= 2:
                    sp.wait_ge(flipped, t - 1)
                c = 0
                for s in sources:
                    sp.dma_start(x[t % 2][:, c:c + s.shape[1]], rows(s)[:, t, :]).then_inc(loaded[t % 2], 16)
                    c += s.shape[1]

        @block.tensor
        def _(pe):
            for t in range(NT):
                pe.wait_ge(loaded[t % 2], 16 * len(sources) * (t // 2 + 1))
                if t >= 2:
                    pe.wait_ge(copied, t - 1)
                for k in range(K):
                    last = nc.tensor.transpose(ps[t % 2][:, k, :], x[t % 2][:, k * P:(k + 1) * P], g.ident[:, :])
                last.then_inc(flipped, 1)

        @block.scalar
        def _(act):
            for t in range(NT):
                act.wait_ge(flipped, t + 1)
                nc.scalar.copy(T[:, :, t * P:(t + 1) * P], ps[t % 2][:, :, :]).then_inc(copied, 1)


def merge(nc, g, T):
    K = W // P
    with stage(nc, g) as ctx:
        sb = lambda n, shape: ctx.enter_context(nc.sbuf_tensor("mg_" + n, shape, F32))
        w = sb("w", [P, 2, K, D])
        bias = sb("bias", [P, 2, D])
        gate = [sb(f"gate{b}", [P, 2, CH]) for b in range(2)]
        sig = [sb(f"sig{b}", [P, 2, CH]) for b in range(2)]
        out = [sb(f"out{b}", [P, CH]) for b in range(2)]
        ps = [[ctx.enter_context(nc.psum_tensor(f"mg_ps{b}{s}", [P, CH], F32)) for s in range(2)] for b in range(2)]
        small, product, biased = g.sem("mg_small"), g.sem("mg_product"), g.sem("mg_biased")
        loaded = [g.sem(f"mg_loaded{b}") for b in range(2)]
        sigmoid, mixed = g.sem("mg_sigmoid"), g.sem("mg_mixed")
        stored = [g.swdge_sem(f"mg_stored{b}") for b in range(2)]
        jobs = [(t, c) for c in range(0, D, CH) for t in range(NT)]
        block = ctx.enter_context(nc.Block())

        @block.sync
        def _(sp):
            for s, v in enumerate((g.d["w_proj_fox"][0], g.d["w_proj_dsa"][0])):
                sp.dma_start(w[:, s, :, :], v.rearrange("(k p) n -> p k n", p=P)).then_inc(small, 16)
            sp.dma_start(bias[:, :, :].rearrange("p a b -> p (a b)"), row_bcast(g.d["b_gate"][0], 2 * D)).then_inc(small, 16)
            for n, (t, c) in enumerate(jobs):
                if n >= 2:
                    sp.wait_ge(sigmoid, n - 1)
                for s in range(2):
                    a = C_GATE + s * D + c
                    sp.dma_start(gate[n % 2][:, s, :], rows(g.d["proj1"])[:, t, a:a + CH]).then_inc(loaded[n % 2], 16)

        @block.gpsimd
        def _(pool):
            for n, (t, c) in enumerate(jobs):
                pool.wait_ge(mixed, n + 1)
                pool.dma_start(rows(g.d["merged"])[:, t, c:c + CH], out[n % 2][:, :]).then_inc(stored[n % 2], 16)
            for b in range(2):
                pool.wait_ge(stored[b], 16 * len(jobs) // 2)

        @block.tensor
        def _(pe):
            pe.wait_ge(small, 48)
            for n, (t, c) in enumerate(jobs):
                if n >= 2:
                    pe.wait_ge(mixed, n - 1)
                for s in range(2):
                    for k in range(K):
                        last = nc.tensor.matmul(ps[n % 2][s][:, :], T[:, s * K + k, t * P:(t + 1) * P], w[:, s, k, c:c + CH], start=k == 0, stop=k == K - 1)
                last.then_inc(product, 1)

        @block.scalar
        def _(act):
            for n, (t, c) in enumerate(jobs):
                act.wait_ge(biased, n + 1)
                if n >= 2:
                    act.wait_ge(mixed, n - 1)
                nc.scalar.activation(sig[n % 2][:, :, :], gate[n % 2][:, :, :], ACT.Sigmoid).then_inc(sigmoid, 1)

        @block.vector
        def _(dve):
            chain = g.chain(dve)
            dve.wait_ge(small, 48)
            for n in range(-1, len(jobs)):
                if n + 1 < len(jobs):
                    m = n + 1
                    dve.wait_ge(loaded[m % 2], 32 * (m // 2 + 1))
                    c = jobs[m][1]
                    nc.vector.tensor_tensor(gate[m % 2][:, :, :], gate[m % 2][:, :, :], bias[:, :, c:c + CH], ALU.add).then_inc(biased, 1)
                if n >= 0:
                    dve.wait_ge(sigmoid, n + 1)
                    dve.wait_ge(product, n + 1)
                    if n >= 2:
                        dve.wait_ge(stored[n % 2], 16 * (n // 2))
                    chain(nc.vector.tensor_tensor(out[n % 2][:, :], sig[n % 2][:, 0, :], ps[n % 2][0][:, :], ALU.mult))
                    chain(nc.vector.tensor_tensor(sig[n % 2][:, 1, :], sig[n % 2][:, 1, :], ps[n % 2][1][:, :], ALU.mult))
                    nc.vector.tensor_tensor(out[n % 2][:, :], out[n % 2][:, :], sig[n % 2][:, 1, :], ALU.add).then_inc(mixed, 1)


def project_residual(nc, g, name, T, w_dram, x_dram, gate_col, out_dram, width=CH):
    K = T.shape[1]
    with stage(nc, g) as ctx:
        sb = lambda n, shape: ctx.enter_context(nc.sbuf_tensor(name + n, shape, F32))
        w = [sb(f"w{b}", [P, K, width]) for b in range(2)]
        gate = sb("gate", [P, D])
        x = [sb(f"x{b}", [P, width]) for b in range(2)]
        out = [sb(f"out{b}", [P, width]) for b in range(2)]
        ps = [ctx.enter_context(nc.psum_tensor(f"{name}ps{b}", [P, CH], F32)) for b in range(2)]
        g_ps = [ctx.enter_context(nc.psum_tensor(f"{name}g{b}", [P, CH], F32)) for b in range(2)]
        loaded = [g.sem(name + f"loaded{b}") for b in range(2)]
        x_loaded = [g.swdge_sem(name + f"x_loaded{b}") for b in range(2)]
        gate_row = g.sem(name + "gate_row")
        product, added = g.sem(name + "product"), g.sem(name + "added")
        stored = [g.swdge_sem(name + f"stored{b}") for b in range(2)]
        jobs = [(t, c) for c in range(0, D, width) for t in range(NT)]
        w_v = w_dram.rearrange("(k p) n -> p k n", p=P)
        block = ctx.enter_context(nc.Block())

        @block.sync
        def _(sp):
            for c in range(D // width):
                if c >= 2:
                    sp.wait_ge(product, NT * (c - 1))
                sp.dma_start(w[c % 2][:, :, :], w_v[:, :, c * width:(c + 1) * width]).then_inc(loaded[c % 2], 16)

        @block.gpsimd
        def _(pool):
            for n in range(len(jobs) + 1):
                if n < len(jobs):
                    t, c = jobs[n]
                    if n >= 2:
                        pool.wait_ge(added, n - 1)
                    pool.dma_start(x[n % 2][:, :], rows(x_dram)[:, t, c:c + width]).then_inc(x_loaded[n % 2], 16)
                if n >= 1:
                    t, c = jobs[n - 1]
                    pool.wait_ge(added, n)
                    pool.dma_start(rows(out_dram)[:, t, c:c + width], out[(n - 1) % 2][:, :]).then_inc(stored[(n - 1) % 2], 16)
            for b in range(2):
                pool.wait_ge(stored[b], 16 * len(jobs) // 2)

        @block.tensor
        def _(pe):
            for k in range(KD):
                col = g.modT[:, gate_col + k:gate_col + k + 1].broadcast_to([P, P])
                last = nc.tensor.matmul(g_ps[k // 4][:, (k % 4) * P:(k % 4 + 1) * P], col, g.ident[:, :], start=True, stop=True)
            last.then_inc(gate_row, 1)
            for n, (t, c) in enumerate(jobs):
                if t == 0:
                    pe.wait_ge(loaded[(c // width) % 2], 16 * (c // width // 2 + 1))
                if n >= 2:
                    pe.wait_ge(added, n - 1)
                for k in range(K):
                    last = nc.tensor.matmul(ps[n % 2][:, 0:width], T[:, k, t * P:(t + 1) * P], w[(c // width) % 2][:, k, :], start=k == 0, stop=k == K - 1)
                last.then_inc(product, 1)

        @block.vector
        def _(dve):
            chain = g.chain(dve)
            dve.wait_ge(gate_row, 1)
            nc.vector.tensor_copy(gate[:, 0:CH], g_ps[0][:, :])
            chain(nc.vector.tensor_copy(gate[:, CH:D], g_ps[1][:, :]))
            for n, (t, c) in enumerate(jobs):
                dve.wait_ge(product, n + 1)
                dve.wait_ge(x_loaded[n % 2], 16 * (n // 2 + 1))
                if n >= 2:
                    dve.wait_ge(stored[n % 2], 16 * (n // 2))
                chain(nc.vector.tensor_tensor(out[n % 2][:, :], ps[n % 2][:, 0:width], gate[:, c:c + width], ALU.mult))
                nc.vector.tensor_tensor(out[n % 2][:, :], out[n % 2][:, :], x[n % 2][:, :], ALU.add).then_inc(added, 1)


NG, EG, NE, F = 4, 8, 32, 512
SLOTS = 2 * S
BLOCKS = NE + (SLOTS - NE) // P
TABLE = BLOCKS + 3


def route(nc, g, hT):
    R = NG + NE
    with stage(nc, g) as ctx:
        sb = lambda n, shape, dt=F32: ctx.enter_context(nc.sbuf_tensor("rt_" + n, shape, dt))
        w = sb("w", [P, KD, R])
        bias = sb("bias", [P, R])
        L = sb("L", [P, NT, R])
        pick = sb("pick", [P, NE])
        tri, ones = sb("tri", [P, P]), sb("ones", [P, P])
        gm, gs = sb("gm", [P, NT]), sb("gs", [P, NT])
        t4, o4 = sb("t4", [P, NT, NG]), sb("o4", [P, NT, NG])
        t32, o1, o2 = sb("t32", [P, NT, NE]), sb("o1", [P, NT, NE]), sb("o2", [P, NT, NE])
        m1, m2 = sb("m1", [P, NT]), sb("m2", [P, NT])
        p1, p2 = sb("p1", [P, NT]), sb("p2", [P, NT])
        rank = sb("rank", [P, NT, NE])
        count, nblk, start, end = sb("count", [P, NE]), sb("nblk", [P, NE]), sb("start", [P, NE]), sb("end", [P, NE])
        tmp = sb("tmp", [P, NE])
        pad = sb("pad", [P, TABLE, 4], I32)
        pos = sb("pos", [P, NT, 2], F32)
        pos_i = sb("pos_i", [P, NT, 2], I32)
        slot = sb("slot", [P, NT, 2, 4], I32)
        slot_f = slot[:, :, :, :].bitcast(F32)
        bnum = sb("bnum", [1, 64])
        bcmp = sb("bcmp", [1, 64, NE])
        bexp = sb("bexp", [1, 64])
        l_ps = [ctx.enter_context(nc.psum_tensor(f"rt_l{b}", [P, CH], F32)) for b in range(2)]
        c_ps = ctx.enter_context(nc.psum_tensor("rt_c", [P, CH], F32))
        o_ps = ctx.enter_context(nc.psum_tensor("rt_o", [P, CH], F32))
        small, padded = g.sem("rt_small"), g.swdge_sem("rt_padded")
        logits, taken = g.sem("rt_logits"), g.sem("rt_taken")
        to_exp, from_exp = g.sem("rt_to_exp"), g.sem("rt_from_exp")
        onehot, counted = g.sem("rt_onehot"), g.sem("rt_counted")
        ready, scattered = g.sem("rt_ready"), g.swdge_sem("rt_scattered")
        iota = g.sem("rt_iota")
        smalls = [(w[:, :, 0:NG], g.d["router_w_grp"][0].rearrange("(k p) n -> p k n", p=P)),
                  (w[:, :, NG:R], g.d["router_w_exp"][0].rearrange("(k p) n -> p k n", p=P)),
                  (bias[:, 0:NG], row_bcast(g.d["router_b_grp"][0], NG)), (bias[:, NG:R], row_bcast(g.d["router_b_exp"][0], NE)),
                  (pick[:, :], row_bcast(g.d["c_pick"], NE)), (tri[:, :], g.d["c_tri_strict"])]
        block = ctx.enter_context(nc.Block())

        @block.sync
        def _(sp):
            for dst, src in smalls:
                sp.dma_start(dst, src).then_inc(small, 16)

        @block.tensor
        def _(pe):
            pe.wait_ge(small, 16 * len(smalls))
            for t in range(NT):
                if t >= 2:
                    pe.wait_ge(taken, t - 1)
                for k in range(KD):
                    last = nc.tensor.matmul(l_ps[t % 2][:, 0:R], hT[:, k, t * P:(t + 1) * P], w[:, k, :], start=k == 0, stop=k == KD - 1)
                last.then_inc(logits, 1)
            pe.wait_ge(onehot, 1)
            v = t32[:, :, :].rearrange("p a b -> p (a b)")
            nc.tensor.matmul(c_ps[:, 0:NT * NE], tri[:, :], v, start=True, stop=True)
            nc.tensor.matmul(o_ps[:, 0:NT * NE], ones[:, :], v, start=True, stop=True).then_inc(counted, 1)

        @block.scalar
        def _(act):
            act.wait_ge(to_exp, 1)
            nc.scalar.activation(t4[:, :, :], t4[:, :, :], ACT.Exp).then_inc(from_exp, 1)
            act.wait_ge(to_exp, 2)
            nc.scalar.activation(p2[:, :], p2[:, :], ACT.Exp).then_inc(from_exp, 1)

        @block.gpsimd
        def _(pool):
            chain = g.chain(pool)
            chain(nc.gpsimd.memset(pad[:, :, :], 0))
            nc.gpsimd.iota(pad[:, :, 1:2], [[0, TABLE], [0, 1]], base=SLOTS, channel_multiplier=1).then_inc(iota, 1)
            nc.gpsimd.iota(slot[:, :, :, 0:1], [[P, NT], [0, 2], [0, 1]], base=0, channel_multiplier=1).then_inc(iota, 1)
            nc.gpsimd.iota(slot[:, :, :, 1:2], [[2 * P, NT], [1, 2], [0, 1]], base=0, channel_multiplier=2).then_inc(iota, 1)
            nc.gpsimd.iota(bnum[:, :], [[1, 64]], base=0, channel_multiplier=0, allow_small_or_imprecise_dtypes=True).then_inc(iota, 1)
            pool.wait_ge(iota, 4)
            pool.dma_start(g.d["table"].rearrange("(b p) c -> p b c", p=P), pad[:, :, :]).then_inc(padded, 16)
            pool.wait_ge(padded, 16)
            pool.wait_ge(ready, 1)
            for t in range(NT):
                for j in range(2):
                    pool.indirect_dma_start(g.d["table"], bass.IndirectOffsetOnAxis(pos_i[:, t, j:j + 1].bitcast(U32), 0),
                                            slot[:, t, j, :], None).then_inc(scattered, 16)
            pool.wait_ge(scattered, 16 * 2 * NT)

        @block.vector
        def _(dve):
            chain = g.chain(dve)
            V, TT, TS = nc.vector, nc.vector.tensor_tensor, nc.vector.tensor_scalar
            col = lambda a, n: a[:, :].unsqueeze(2).broadcast_to([P, NT, n])
            row = lambda a, n: a.unsqueeze(1).broadcast_to([P, NT, n])
            chain(V.memset(ones[:, :], 1.0))
            dve.wait_ge(small, 16 * len(smalls))
            for t in range(NT):
                dve.wait_ge(logits, t + 1)
                TT(L[:, t, :], l_ps[t % 2][:, 0:R], bias[:, :], ALU.add).then_inc(taken, 1)
            dve.wait_ge(taken, NT)

            def first_max(x, m, out, n):
                chain(V.tensor_reduce(m[:, :], x, AX, ALU.max))
                chain(TT(out, x, col(m, n), ALU.is_equal))
                chain(TT(out, out, row(pick[:, 0:n], n), ALU.mult))
                chain(V.tensor_reduce(gs[:, :], out, AX, ALU.max))
                chain(TT(out, out, col(gs, n), ALU.is_equal))
            first_max(L[:, :, 0:NG], gm, o4[:, :, :], NG)
            TT(t4[:, :, :], L[:, :, 0:NG], col(gm, NG), ALU.subtract).then_inc(to_exp, 1)
            chain(TS(o4[:, :, :], o4[:, :, :], 1.0, -NEG, ALU.subtract, ALU.mult))
            EL = L[:, :, NG:R]
            for q in range(NG):
                chain(TT(EL[:, :, q * EG:(q + 1) * EG], EL[:, :, q * EG:(q + 1) * EG], o4[:, :, q:q + 1].broadcast_to([P, NT, EG]), ALU.add))
            first_max(EL, m1, o1[:, :, :], NE)
            chain(TS(t32[:, :, :], o1[:, :, :], 2 * NEG, None, ALU.mult))
            chain(TT(EL, EL, t32[:, :, :], ALU.add))
            first_max(EL, m2, o2[:, :, :], NE)
            TT(p2[:, :], m2[:, :], m1[:, :], ALU.subtract).then_inc(to_exp, 1)
            TT(t32[:, :, :], o1[:, :, :], o2[:, :, :], ALU.add).then_inc(onehot, 1)
            dve.wait_ge(from_exp, 2)
            chain(V.tensor_reduce(gs[:, :], t4[:, :, :], AX, ALU.add))
            chain(TS(p1[:, :], p2[:, :], 1.0, None, ALU.add))
            chain(TT(gs[:, :], gs[:, :], p1[:, :], ALU.mult))
            chain(V.reciprocal(p1[:, :], gs[:, :]))
            chain(TT(p2[:, :], p2[:, :], p1[:, :], ALU.mult))
            dve.wait_ge(iota, 4)
            chain(V.tensor_copy(slot_f[:, :, 0, 2], p1[:, :]))
            chain(V.tensor_copy(slot_f[:, :, 1, 2], p2[:, :]))
            chain(V.memset(slot[:, :, :, 3:4], 0))
            dve.wait_ge(counted, 1)
            chain(V.memset(count[:, :], 0.0))
            for t in range(NT):
                chain(TT(rank[:, t, :], c_ps[:, t * NE:(t + 1) * NE], count[:, :], ALU.add))
                chain(TT(count[:, :], count[:, :], o_ps[:, t * NE:(t + 1) * NE], ALU.add))
            chain(TS(nblk[:, :], count[:, :], 0.5, None, ALU.is_gt))
            for k in range(1, NT):
                chain(TS(tmp[:, :], count[:, :], k * P + 0.5, None, ALU.is_gt))
                chain(TT(nblk[:, :], nblk[:, :], tmp[:, :], ALU.add))
            chain(V.memset(tmp[:, :], 1.0))
            chain(V.tensor_tensor_scan(end[:, :], tmp[:, :], nblk[:, :], 0.0, ALU.mult, ALU.add))
            chain(TT(start[:, :], end[:, :], nblk[:, :], ALU.subtract))
            chain(TS(start[:, :], start[:, :], float(P), None, ALU.mult))
            chain(TT(rank[:, :, :], rank[:, :, :], row(start[:, :], NE), ALU.add))
            for j, o in enumerate((o1, o2)):
                chain(TT(t32[:, :, :], rank[:, :, :], o[:, :, :], ALU.mult))
                chain(V.tensor_reduce(pos[:, :, j:j + 1], t32[:, :, :], AX, ALU.add))
            V.tensor_copy(pos_i[:, :, :], pos[:, :, :]).then_inc(ready, 1)
            chain(TT(bcmp[:, :, :], end[0:1, :].unsqueeze(1).broadcast_to([1, 64, NE]), bnum[:, :].unsqueeze(2).broadcast_to([1, 64, NE]), ALU.is_le))
            chain(V.tensor_reduce(bexp[:, :], bcmp[:, :, :], AX, ALU.add))
            chain(TS(bexp[:, :], bexp[:, :], float(NE - 1), None, ALU.min))
            chain(TS(bexp[:, 63:64], end[0:1, NE - 1:NE], 0.5, 0.25, ALU.mult, ALU.add))
            chain(V.tensor_copy(g.experts[:, :], bexp[:, :]))


def experts(nc, g):
    with stage(nc, g) as ctx:
        sb = lambda n, shape, dt=F32: ctx.enter_context(nc.sbuf_tensor("ex_" + n, shape, dt))
        w13 = [sb(f"w13_{b}", [P, 2, KD, F]) for b in range(2)]
        w2 = [sb(f"w2_{b}", [P, F // P, D]) for b in range(2)]
        entries = sb("entries", [P, TABLE, 4], I32)
        entry = [sb(f"entry{b}", [P, 4], I32) for b in range(2)]
        to_gather = [sb(f"to_gather{b}", [P, 4], I32) for b in range(2)]
        x = [sb(f"x{b}", [P, D]) for b in range(2)]
        xT = [sb(f"xT{b}", [P, KD, P]) for b in range(2)]
        gain = sb("gain", [P, KD])
        act_s, act_t = sb("silu", [P, F]), sb("act", [P, F])
        actT = sb("actT", [P, F // P, P])
        y = [sb(f"y{b}", [P, D]) for b in range(2)]
        x_ps = ctx.enter_context(nc.psum_tensor("ex_x", [P, KD, P], F32))
        a_ps = ctx.enter_context(nc.psum_tensor("ex_a", [P, F], F32))
        b_ps = ctx.enter_context(nc.psum_tensor("ex_b", [P, F], F32))
        t_ps = ctx.enter_context(nc.psum_tensor("ex_t", [P, F // P, P], F32))
        y_ps = ctx.enter_context(nc.psum_tensor("ex_y", [P, D], F32))
        sem = lambda n: g.sem("ex_" + n)
        passed = sem("passed")
        w_loaded = [sem(f"w_loaded{b}") for b in range(2)]
        entries_loaded, copied_g, copied_s = g.swdge_sem("ex_entries_loaded"), sem("copied_g"), sem("copied_s")
        gathered = [g.swdge_sem(f"ex_gathered{b}") for b in range(2)]
        scattered = [g.swdge_sem(f"ex_scattered{b}") for b in range(2)]
        x_flipped, x_ready = sem("x_flipped"), sem("x_ready")
        ab, silu, acted = sem("ab"), sem("silu"), sem("acted")
        a_flipped, a_ready = sem("a_flipped"), sem("a_ready")
        y_done, y_ready, gain_ready = sem("y_done"), sem("y_ready"), sem("gain_ready")
        shift = g.modT[:, 24:24 + KD]
        table_v = g.d["table"].rearrange("(b p) c -> p b c", p=P)
        pairs = lambda eng: eng.value_load(g.experts[0:1, 63:64], min_val=1, max_val=(BLOCKS + 1) // 2)
        block = ctx.enter_context(nc.Block())

        @block.sync
        def _(sp):
            n_pairs = pairs(sp)
            with sp.Fori(0, n_pairs) as i:
                for b in range(2):
                    expert = sp.value_load(g.experts[0:1, bass.ds(i * 2 + b, 1)], min_val=0, max_val=NE - 1)
                    sp.wait_ge(y_done, i * 2 + b)
                    for s, wd in enumerate((g.d["exp_w1"], g.d["exp_w3"])):
                        src = wd[0].rearrange("e (k p) f -> p e k f", p=P)[:, bass.ds(expert, 1), :, :]
                        sp.dma_start(w13[b][:, s:s + 1, :, :], src).then_inc(w_loaded[b], 16)
                    src = g.d["exp_w2"][0].rearrange("e (k p) f -> p e k f", p=P)[:, bass.ds(expert, 1), :, :]
                    sp.dma_start(w2[b][:, :, :].unsqueeze(1), src).then_inc(w_loaded[b], 16)

        @block.gpsimd
        def _(pool):
            n_pairs = pairs(pool)
            pool.dma_start(entries[:, :, :], table_v).then_inc(entries_loaded, 16)
            pool.wait_ge(entries_loaded, 16)
            pool.sem_inc(x_flipped, 1)

            def gather(n, b):
                nc.gpsimd.tensor_copy(to_gather[b][:, :].unsqueeze(1), entries[:, bass.ds(n, 1), :]).then_inc(copied_g, 1)
                pool.wait_ge(copied_g, n + 1)
                pool.sem_inc(passed, 1)
                pool.indirect_dma_start(x[b][:, :], None, g.d["xn2"], bass.IndirectOffsetOnAxis(to_gather[b][:, 0:1].bitcast(U32), 0)).then_inc(gathered[b], 16)

            gather(0, 0)
            gather(1, 1)
            with pool.Fori(0, n_pairs) as i:
                for b in range(2):
                    pool.wait_ge(scattered[b], i * 16)
                    nc.gpsimd.tensor_copy(entry[b][:, :].unsqueeze(1), entries[:, bass.ds(i * 2 + b, 1), :]).then_inc(copied_s, 1)
                    pool.wait_ge(x_flipped, i * 2 + (b + 2))
                    gather(i * 2 + (b + 2), b)
                    pool.wait_ge(scattered[1 - b], (i + b) * 16)
                    pool.wait_ge(y_ready, i * 2 + (b + 1))
                    pool.sem_inc(passed, 1)
                    pool.indirect_dma_start(g.d["moe_y"], bass.IndirectOffsetOnAxis(entry[b][:, 1:2].bitcast(U32), 0), y[b][:, :], None).then_inc(scattered[b], 16)
            for b in range(2):
                pool.wait_ge(gathered[b], n_pairs * 16 + 16)
                pool.wait_ge(scattered[b], n_pairs * 16)

        @block.tensor
        def _(pe):
            n_pairs = pairs(pe)
            pe.sem_inc(y_done, 1)

            def flip_x(n, count, b):
                pe.wait_ge(gathered[b], (count + 1) * 16)
                pe.wait_ge(x_ready, n)
                for k in range(KD):
                    last = nc.tensor.transpose(x_ps[:, k, :], x[b][:, k * P:(k + 1) * P], g.ident[:, :])
                last.then_inc(x_flipped, 1)

            flip_x(0, 0, 0)
            with pe.Fori(0, n_pairs) as i:
                for b in range(2):
                    n = i * 2 + b
                    pe.wait_ge(w_loaded[b], i * 48 + 48)
                    pe.wait_ge(x_ready, i * 2 + (b + 1))
                    pe.wait_ge(acted, n)
                    for s, ps in enumerate((a_ps, b_ps)):
                        for k in range(KD):
                            last = nc.tensor.matmul(ps[:, :], xT[b][:, k, :], w13[b][:, s, k, :], start=k == 0, stop=k == KD - 1)
                    last.then_inc(ab, 1)
                    flip_x(i * 2 + (b + 1), i + b, 1 - b)
                    pe.wait_ge(acted, i * 2 + (b + 1))
                    for k in range(F // P):
                        last = nc.tensor.transpose(t_ps[:, k, :], act_t[:, k * P:(k + 1) * P], g.ident[:, :])
                    last.then_inc(a_flipped, 1)
                    pe.wait_ge(a_ready, i * 2 + (b + 1))
                    pe.wait_ge(y_ready, n)
                    for c in range(0, D, CH):
                        for k in range(F // P):
                            last = nc.tensor.matmul(y_ps[:, c:c + CH], actT[:, k, :], w2[b][:, k, c:c + CH], start=k == 0, stop=k == F // P - 1)
                    last.then_inc(y_done, 1)

        @block.scalar
        def _(act):
            n_pairs = pairs(act)

            def copy_x(n1, count1, b):
                act.wait_ge(x_flipped, n1)
                for k in range(KD):
                    last = nc.scalar.activation(xT[b][:, k, :], x_ps[:, k, :], ACT.Identity, bias=shift[:, k:k + 1], scale=gain[:, k:k + 1])
                last.then_inc(x_ready, 1)

            act.wait_ge(gain_ready, 1)
            copy_x(2, 0, 0)
            with act.Fori(0, n_pairs) as i:
                for b in range(2):
                    act.wait_ge(ab, i * 2 + (b + 1))
                    act.wait_ge(acted, i * 2 + b)
                    nc.scalar.activation(act_s[:, :], a_ps[:, :], ACT.Silu).then_inc(silu, 1)
                    copy_x(i * 2 + (b + 3), 0, 1 - b)
                    act.wait_ge(a_flipped, i * 2 + (b + 1))
                    nc.scalar.copy(actT[:, :, :], t_ps[:, :, :]).then_inc(a_ready, 1)

        @block.vector
        def _(dve):
            chain = g.chain(dve)
            n_pairs = pairs(dve)
            chain(nc.vector.tensor_scalar(gain[:, :], g.modT[:, 24 + KD:24 + 2 * KD], 1.0, None, ALU.add))
            nc.vector.tensor_tensor(gain[:, :], gain[:, :], g.gainT[:, KD:2 * KD], ALU.mult).then_inc(gain_ready, 1)
            with dve.Fori(0, n_pairs) as i:
                for b in range(2):
                    dve.wait_ge(silu, i * 2 + (b + 1))
                    dve.wait_ge(a_flipped, i * 2 + b)
                    nc.vector.tensor_tensor(act_t[:, :], act_s[:, :], b_ps[:, :], ALU.mult).then_inc(acted, 1)
                    dve.wait_ge(y_done, i * 2 + (b + 2))
                    dve.wait_ge(copied_s, i * 2 + (b + 1))
                    nc.vector.tensor_scalar(y[b][:, :], y_ps[:, :], entry[b][:, 2:3].bitcast(F32), None, ALU.mult).then_inc(y_ready, 1)


def combine(nc, g):
    with stage(nc, g) as ctx:
        sb = lambda n, shape: ctx.enter_context(nc.sbuf_tensor("cb_" + n, shape, F32))
        y = [sb(f"y{b}", [P, 2, D]) for b in range(2)]
        x = [sb(f"x{b}", [P, D]) for b in range(2)]
        gate = sb("gate", [P, D])
        g_ps = ctx.enter_context(nc.psum_tensor("cb_g", [P, D], F32))
        loaded = [g.sem(f"cb_loaded{b}") for b in range(2)]
        stored = [g.sem(f"cb_stored{b}") for b in range(2)]
        gate_row, added = g.sem("cb_gate_row"), g.sem("cb_added")
        y_v = g.d["moe_y"][0:SLOTS, :].rearrange("(t p j) n -> p t j n", p=P, j=2)
        block = ctx.enter_context(nc.Block())

        @block.sync
        def _(sp):
            for t in range(NT):
                if t >= 2:
                    sp.wait_ge(stored[t % 2], 16 * (t // 2))
                sp.dma_start(y[t % 2][:, :, :], y_v[:, t, :, :]).then_inc(loaded[t % 2], 16)
                sp.dma_start(x[t % 2][:, :], rows(g.d["x1"])[:, t, :]).then_inc(loaded[t % 2], 16)

        @block.scalar
        def _(act):
            for t in range(NT):
                act.wait_ge(added, t + 1)
                act.dma_start(rows(g.d["x2"])[:, t, :], x[t % 2][:, :]).then_inc(stored[t % 2], 16)
            for b in range(2):
                act.wait_ge(stored[b], 16 * (NT // 2))

        @block.tensor
        def _(pe):
            for k in range(KD):
                col = g.modT[:, 5 * KD + k:5 * KD + k + 1].broadcast_to([P, P])
                last = nc.tensor.matmul(g_ps[:, k * P:(k + 1) * P], col, g.ident[:, :], start=True, stop=True)
            last.then_inc(gate_row, 1)

        @block.vector
        def _(dve):
            chain = g.chain(dve)
            dve.wait_ge(gate_row, 1)
            chain(nc.vector.tensor_copy(gate[:, :], g_ps[:, :]))
            for t in range(NT):
                a = y[t % 2]
                dve.wait_ge(loaded[t % 2], 32 * (t // 2 + 1))
                chain(nc.vector.tensor_tensor(a[:, 0, :], a[:, 0, :], a[:, 1, :], ALU.add))
                chain(nc.vector.tensor_tensor(a[:, 0, :], a[:, 0, :], gate[:, :], ALU.mult))
                nc.vector.tensor_tensor(x[t % 2][:, :], x[t % 2][:, :], a[:, 0, :], ALU.add).then_inc(added, 1)


def flip_heads(nc, g, name, src, pairs, q16T):
    with stage(nc, g) as ctx:
        x = [ctx.enter_context(nc.sbuf_tensor(f"{name}x{b}", [P, 2 * W], F32)) for b in range(2)]
        ps = [ctx.enter_context(nc.psum_tensor(f"{name}ps{b}", [DH, 4, P], F32)) for b in range(4)]
        loaded = [g.sem(name + f"loaded{b}") for b in range(2)]
        flipped, copied = g.sem(name + "flipped"), g.sem(name + "copied")
        block = ctx.enter_context(nc.Block())

        @block.sync
        def _(sp):
            for t in range(NT):
                if t >= 2:
                    sp.wait_ge(flipped, 4 * (t - 1))
                sp.dma_start(x[t % 2][:, :], rows(src)[:, t, :]).then_inc(loaded[t % 2], 16)

        @block.tensor
        def _(pe):
            for t in range(NT):
                pe.wait_ge(loaded[t % 2], 16 * (t // 2 + 1))
                for n in range(4 * t, 4 * t + 4):
                    if n >= 4:
                        pe.wait_ge(copied, n - 3)
                    for j in range(4):
                        c = (4 * (n % 4) + j) * DH
                        last = nc.tensor.transpose(ps[n % 4][:, j, :], x[t % 2][:, c:c + DH], g.ident[:, :])
                    last.then_inc(flipped, 1)

        @block.scalar
        def _(act):
            for t in range(NT):
                for n in range(4 * t, 4 * t + 4):
                    act.wait_ge(flipped, n + 1)
                    to, scale = pairs[n % 4 // 2]
                    h = 4 * (n % 2)
                    nc.scalar.mul(to[:, h:h + 4, t * P:(t + 1) * P], ps[n % 4][:, :, :], scale).then_inc(copied, 1)
            act.wait_ge(copied, 4 * NT)
            for h in range(H):
                nc.scalar.copy(q16T[:, h, :].rearrange("d (r m) -> d r m", r=16),
                               pairs[0][0][:, h, :].rearrange("d (m r) -> d r m", r=16))


BRANCHES = 3
SPAN = 3 * P - 1


def bias_tables(nc, g, tables):
    with stage(nc, g) as ctx:
        sb = lambda n, shape: ctx.enter_context(nc.sbuf_tensor("bt_" + n, shape, F32))
        rel = sb("rel", [33, H])
        bucket = sb("bucket", [33, BRANCHES, SPAN])
        line = [sb(f"line{b}", [P, H, SPAN]) for b in range(BRANCHES)]
        ps = [ctx.enter_context(nc.psum_tensor(f"bt_ps{b}", [P, CH], F32)) for b in range(2)]
        small, masked = g.sem("bt_small"), g.sem("bt_masked")
        picked, copied = g.sem("bt_picked"), g.sem("bt_copied")
        written, read = g.sem("bt_written"), g.sem("bt_read")
        skew = g.d["skew"]
        jobs = [(r, h) for r in range(BRANCHES) for h in range(H)]
        block = ctx.enter_context(nc.Block())

        @block.sync
        def _(sp):
            sp.dma_start(rel[0:32, :], g.d["rel_bias_2"]).then_inc(small, 16)
            sp.dma_start(bucket[:, :, :], g.d["c_bucket"]).then_inc(small, 16)
            for r in range(BRANCHES):
                sp.wait_ge(copied, H * (r + 1))
                sp.dma_start(skew[r].rearrange("h (p n) -> p h n", n=SPAN), line[r][:, :, :]).then_inc(written, 16)
            sp.wait_ge(written, 16 * BRANCHES)
            sp.wait_ge(masked, 2)
            for r in range(BRANCHES):
                back = skew[r][:, P - 1:P - 1 + P * (SPAN - 1)].rearrange("h (p n) -> p h n", n=SPAN - 1)
                if r < 2:
                    sp.dma_start(tables[r][:, :, :], back[:, :, 0:2 * P]).then_inc(read, 16)
                else:
                    for half in range(2):
                        a = slice(half * DH, (half + 1) * DH)
                        sp.dma_start(tables[r][a, :, a], back[0:DH, :, P:P + DH]).then_inc(read, 16)
            sp.wait_ge(read, 64)

        @block.tensor
        def _(pe):
            pe.wait_ge(small, 32)
            pe.wait_ge(masked, 1)
            for n, (r, h) in enumerate(jobs):
                if n >= 2:
                    pe.wait_ge(copied, n - 1)
                nc.tensor.matmul(ps[n % 2][:, 0:SPAN], rel[:, h:h + 1].broadcast_to([33, P]), bucket[:, r, :], start=True, stop=True).then_inc(picked, 1)

        @block.vector
        def _(dve):
            nc.vector.memset(rel[32:33, :], NEG).then_inc(masked, 1)
            nc.vector.memset(tables[2][:, :, :], NEG).then_inc(masked, 1)
            for n, (r, h) in enumerate(jobs):
                dve.wait_ge(picked, n + 1)
                nc.vector.tensor_copy(line[r][:, h, :], ps[n % 2][:, 0:SPAN]).then_inc(copied, 1)


def dilated(nc, g):
    with ExitStack() as ctx:
        sb = lambda n, shape: ctx.enter_context(nc.sbuf_tensor("dl_" + n, shape, F32))
        qT, kT, q16T = sb("qT", [DH, H, S]), sb("kT", [DH, H, S]), sb("q16T", [DH, H, S])
        v = [sb(f"v{r}", [P, NT, W]) for r in range(BRANCHES)]
        tables = [sb("bias0", [P, H, 2 * P]), sb("bias1", [P, H, 2 * P]), sb("bias2", [P, H, P])]
        flip_heads(nc, g, "fh", g.d["proj2"][:, C_QA:C_QA + 2 * W], [(qT, DH ** -0.5), (kT, 1.0)], q16T)
        bias_tables(nc, g, tables)
        units, places = [], []
        wide = lambda dram: dram.rearrange("n (h d) -> n h d", d=DH + 2)
        for dil, r in ((1, 0), (4, 1)):
            q_v = qT[:, :, :].rearrange("d h (m r) -> d h r m", r=dil)
            k_v = kT[:, :, :].rearrange("d h (m r) -> d h r m", r=dil)
            for res in range(dil):
                for n in range(NT // dil):
                    lo = max(n - 1, 0)
                    for h in range(H):
                        units.append(Unit(
                            width=(n + 1 - lo) * P, q=q_v[:, h, res, n * P:(n + 1) * P],
                            mask=(tables[r][:, h, :] if n else tables[r][:, h, P:2 * P], 0),
                            k=lambda c, w, h=h, res=res, lo=lo, k_v=k_v: k_v[:, h, res, lo * P + c:lo * P + c + w],
                            v=lambda j, h=h, r=r, at=res * (NT // dil) + lo: v[r][:, at + j, h * DH:(h + 1) * DH]))
                    to = wide(g.d["branch"][r]).rearrange("(n p r) h d -> r n p h d", p=P, r=dil)[res, n]
                    places.append([(to, 0, P)])
        k_v = kT[:, :, :].rearrange("d h (m r) -> d h r m", r=16)
        for n in range(NT):
            for h in range(H):
                units.append(Unit(
                    width=P, q=q16T[:, h, n * P:(n + 1) * P], mask=(tables[2][:, h, :], 0),
                    k=lambda c, w, h=h, n=n: k_v[:, h, 2 * n:2 * n + 2, :],
                    v=lambda j, h=h, n=n: v[2][:, n, h * DH:(h + 1) * DH]))
            to = wide(g.d["branch"][2]).rearrange("(m r) h d -> r m h d", r=16)
            places.append([(to[2 * n], 0, DH), (to[2 * n + 1], DH, P)])
        va = g.d["proj2"][:, C_VA:C_VA + W]
        loads = [(v[0][:, :, :], rows(va))]
        for res in range(4):
            loads.append((v[1][:, 2 * res:2 * res + 2, :], va.rearrange("(n p r) c -> r p n c", p=P, r=4)[res]))
        for half in range(2):
            loads.append((v[2][half * DH:(half + 1) * DH, :, :], va.rearrange("(m n r) c -> r m n c", n=NT, r=2)[half]))
        attention(nc, g, "dil", units, DH + 2, True, lambda n: places[n], loads)
    dilated_merge(nc, g)


def dilated_merge(nc, g):
    with stage(nc, g) as ctx:
        sb = lambda n, shape: ctx.enter_context(nc.sbuf_tensor("dm_" + n, shape, F32))
        x = [sb(f"x{b}", [P, BRANCHES, H, DH + 2]) for b in range(2)]
        a = [sb(f"a{b}", [P, BRANCHES, H]) for b in range(2)]
        low, den, part = sb("low", [P, H]), sb("den", [P, H]), sb("part", [P, H])
        wide = sb("wide", [P, H, DH])
        y = [sb(f"y{b}", [P, H, DH]) for b in range(2)]
        loaded = [g.sem(f"dm_loaded{b}") for b in range(2)]
        stored = [g.swdge_sem(f"dm_stored{b}") for b in range(2)]
        to_exp, exped, merged = g.sem("dm_to_exp"), g.sem("dm_exped"), g.sem("dm_merged")
        block = ctx.enter_context(nc.Block())

        @block.sync
        def _(sp):
            for t in range(NT):
                if t >= 2:
                    sp.wait_ge(merged, t - 1)
                for r in range(BRANCHES):
                    sp.dma_start(x[t % 2][:, r, :, :].rearrange("p h d -> p (h d)"), rows(g.d["branch"][r])[:, t, :]).then_inc(loaded[t % 2], 16)

        @block.gpsimd
        def _(pool):
            for t in range(NT):
                pool.wait_ge(merged, t + 1)
                pool.dma_start(rows(g.d["y_attn"])[:, t, :], y[t % 2][:, :, :].rearrange("p h d -> p (h d)")).then_inc(stored[t % 2], 16)
            for b in range(2):
                pool.wait_ge(stored[b], 16 * (NT // 2))

        @block.scalar
        def _(act):
            for t in range(NT):
                act.wait_ge(to_exp, t + 1)
                nc.scalar.activation(a[t % 2][:, :, :], a[t % 2][:, :, :], ACT.Exp).then_inc(exped, 1)

        @block.vector
        def _(dve):
            chain = g.chain(dve)
            TT = nc.vector.tensor_tensor
            for t in range(NT):
                X, A, Y = x[t % 2], a[t % 2], y[t % 2]
                dve.wait_ge(loaded[t % 2], 48 * (t // 2 + 1))
                nm = lambda r: X[:, r, :, DH]
                chain(TT(low[:, :], nm(0), nm(1), ALU.min))
                chain(TT(low[:, :], low[:, :], nm(2), ALU.min))
                for r in range(BRANCHES):
                    last = TT(A[:, r, :], low[:, :], nm(r), ALU.subtract)
                last.then_inc(to_exp, 1)
                dve.wait_ge(exped, t + 1)
                chain(TT(den[:, :], A[:, 0, :], X[:, 0, :, DH + 1], ALU.mult))
                for r in (1, 2):
                    chain(TT(part[:, :], A[:, r, :], X[:, r, :, DH + 1], ALU.mult))
                    chain(TT(den[:, :], den[:, :], part[:, :], ALU.add))
                chain(nc.vector.reciprocal(den[:, :], den[:, :]))
                if t >= 2:
                    dve.wait_ge(stored[t % 2], 16 * (t // 2))
                by = lambda c: c.unsqueeze(2).broadcast_to([P, H, DH])
                chain(TT(Y[:, :, :], X[:, 0, :, 0:DH], by(A[:, 0, :]), ALU.mult))
                for r in (1, 2):
                    chain(TT(wide[:, :, :], X[:, r, :, 0:DH], by(A[:, r, :]), ALU.mult))
                    chain(TT(Y[:, :, :], Y[:, :, :], wide[:, :, :], ALU.add))
                TT(Y[:, :, :], Y[:, :, :], by(den[:, :]), ALU.mult).then_inc(merged, 1)
                dve.wait_ge(merged, t + 1)


def feed_forward_up(nc, g, hT, actT):
    FT = g.d["w_gate_2"].shape[2] // P
    with stage(nc, g) as ctx:
        sb = lambda n, shape: ctx.enter_context(nc.sbuf_tensor("ff_" + n, shape, F32))
        w = [sb(f"w{b}", [P, 2, KD, P]) for b in range(2)]
        silu = [sb(f"silu{b}", [P, S]) for b in range(2)]
        ps = [[ctx.enter_context(nc.psum_tensor(f"ff_ps{b}{s}", [P, S], F32)) for s in range(2)] for b in range(2)]
        loaded = [g.sem(f"ff_loaded{b}") for b in range(2)]
        product = [g.sem(f"ff_product{b}") for b in range(2)]
        silued = [g.sem(f"ff_silued{b}") for b in range(2)]
        multiplied = [g.sem(f"ff_multiplied{b}") for b in range(2)]
        views = [d[0].rearrange("(k p) n -> p k n", p=P) for d in (g.d["w_gate_2"], g.d["w_up_2"])]
        assert FT % 2 == 0
        block = ctx.enter_context(nc.Block())

        @block.sync
        def _(sp):
            with sp.Fori(0, FT // 2) as i:
                for b in range(2):
                    sp.wait_ge(product[b], i)
                    for s in range(2):
                        sp.dma_start(w[b][:, s, :, :], views[s][:, :, bass.ds(i * (2 * P) + b * P, P)]).then_inc(loaded[b], 16)

        @block.tensor
        def _(pe):
            with pe.Fori(0, FT // 2) as i:
                for b in range(2):
                    pe.wait_ge(loaded[b], i * 32 + 32)
                    pe.wait_ge(multiplied[b], i)
                    for s in range(2):
                        for c in range(0, S, CH):
                            for k in range(KD):
                                last = nc.tensor.matmul(ps[b][s][:, c:c + CH], w[b][:, s, k, :], hT[:, k, c:c + CH], start=k == 0, stop=k == KD - 1)
                    last.then_inc(product[b], 1)

        @block.scalar
        def _(act):
            with act.Fori(0, FT // 2) as i:
                for b in range(2):
                    act.wait_ge(product[b], i + 1)
                    act.wait_ge(multiplied[b], i)
                    nc.scalar.activation(silu[b][:, :], ps[b][0][:, :], ACT.Silu).then_inc(silued[b], 1)

        @block.vector
        def _(dve):
            with dve.Fori(0, FT // 2) as i:
                for b in range(2):
                    dve.wait_ge(silued[b], i + 1)
                    nc.vector.tensor_tensor(actT[:, bass.ds(i * 2 + b, 1), :].rearrange("p a n -> p (a n)"), silu[b][:, :], ps[b][1][:, :], ALU.mult).then_inc(multiplied[b], 1)


def final_norm(nc, g):
    with stage(nc, g) as ctx:
        sb = lambda n, shape: ctx.enter_context(nc.sbuf_tensor("fn_" + n, shape, F32))
        x = [sb(f"x{b}", [P, D]) for b in range(2)]
        square, gain, stat = sb("square", [P, D]), sb("gain", [P, D]), sb("stat", [P, NT])
        loaded = [g.sem(f"fn_loaded{b}") for b in range(2)]
        stored = [g.swdge_sem(f"fn_stored{b}") for b in range(2)]
        small, rooted, done = g.sem("fn_small"), g.sem("fn_rooted"), g.sem("fn_done")
        block = ctx.enter_context(nc.Block())

        @block.sync
        def _(sp):
            sp.dma_start(gain[:, :], row_bcast(g.d["final_norm_g_2"], D)).then_inc(small, 16)
            for t in range(NT):
                if t >= 2:
                    sp.wait_ge(stored[t % 2], 16 * (t // 2))
                sp.dma_start(x[t % 2][:, :], rows(g.d["x4"])[:, t, :]).then_inc(loaded[t % 2], 16)

        @block.gpsimd
        def _(pool):
            for t in range(NT):
                pool.wait_ge(done, t + 1)
                pool.dma_start(rows(g.d["out"])[:, t, :], x[t % 2][:, :]).then_inc(stored[t % 2], 16)
            for b in range(2):
                pool.wait_ge(stored[b], 16 * (NT // 2))

        @block.scalar
        def _(act):
            chain = g.chain(act)
            for t in range(NT):
                act.wait_ge(loaded[t % 2], 16 * (t // 2 + 1))
                chain(nc.scalar.activation(square[:, :], x[t % 2][:, :], ACT.Square, accum_out=stat[:, t:t + 1]))
                nc.scalar.activation(stat[:, t:t + 1], stat[:, t:t + 1], ACT.Sqrt, scale=1.0 / D, bias=g.eps[:, :]).then_inc(rooted, 1)

        @block.vector
        def _(dve):
            chain = g.chain(dve)
            dve.wait_ge(small, 16)
            for t in range(NT):
                dve.wait_ge(rooted, t + 1)
                chain(nc.vector.reciprocal(stat[:, t:t + 1], stat[:, t:t + 1]))
                nc.vector.scalar_tensor_tensor(x[t % 2][:, :], x[t % 2][:, :], stat[:, t:t + 1], gain[:, :], ALU.mult, ALU.mult).then_inc(done, 1)


CK = 64
CONV = 4


def delta_prepare(nc, g, qkv, tab):
    WC = 3 * W
    with stage(nc, g) as ctx:
        sb = lambda n, shape: ctx.enter_context(nc.sbuf_tensor("dp_" + n, shape, F32))
        x = [sb(f"x{b}", [P, CONV, WC]) for b in range(2)]
        taps = sb("taps", [P, CONV, WC])
        square = sb("square", [P, 2 * H, DH])
        stat = sb("stat", [P, 2 * H])
        ab = sb("ab", [P, NT, 2 * H])
        z, t1 = sb("z", [P, NT, H]), sb("t1", [P, NT, H])
        dt, alog = sb("dt", [P, H]), sb("alog", [P, H])
        cum, last_sel, own = sb("cum", [P, P]), sb("last_sel", [P, 2, P]), sb("own", [P, P])
        zeros = sb("zeros", [P, N2])
        c_ps = ctx.enter_context(nc.psum_tensor("dp_c", [P, CH], F32))
        l_ps = [ctx.enter_context(nc.psum_tensor(f"dp_l{b}", [P, CH], F32)) for b in range(3)]
        small, zeroed, padded = g.sem("dp_small"), g.sem("dp_zeroed"), g.sem("dp_padded")
        loaded = [g.sem(f"dp_loaded{b}") for b in range(2)]
        to_act, from_act = g.sem("dp_to_act"), g.sem("dp_from_act")
        g_ready, summed, sum_ready, lasts = g.sem("dp_g_ready"), g.sem("dp_summed"), g.sem("dp_sum_ready"), g.sem("dp_lasts")
        multiplied = g.sem("dp_multiplied")
        convolved, silued = g.sem("dp_convolved"), g.sem("dp_silued")
        squared, rooted, done = g.sem("dp_squared"), g.sem("dp_rooted"), g.sem("dp_done")
        smalls = [(ab[:, :, :], rows(g.d["proj2"])[:, :, C_B:C_B + 2 * H]), (dt[:, :], row_bcast(g.d["dt_bias_2"][0], H)),
                  (alog[:, :], row_bcast(g.d["a_log_2"][0], H)), (cum[:, :], g.d["c_cum64"]),
                  (last_sel[:, :, :], g.d["c_last"][:, 0:2, :]), (own[:, :], g.d["c_last"][:, 2, :]),
                  (taps[:, :, :].rearrange("p a b -> p (a b)"), row_bcast(g.d["conv_w_2"][0].rearrange("a b -> (a b)"), CONV * WC))]
        block = ctx.enter_context(nc.Block())

        @block.sync
        def _(sp):
            for dst, src in smalls:
                sp.dma_start(dst, src).then_inc(small, 16)
            sp.wait_ge(zeroed, 1)
            sp.dma_start(g.d["proj2_padded"][0:CONV - 1, :], zeros[0:CONV - 1, :]).then_inc(padded, 16)
            sp.wait_ge(padded, 16)
            for t in range(NT):
                if t >= 2:
                    sp.wait_ge(convolved, t - 1)
                for j in range(CONV):
                    sp.dma_start(x[t % 2][:, j, :], g.d["proj2_padded"][t * P + j:(t + 1) * P + j, C_QKV:C_QKV + WC]).then_inc(loaded[t % 2], 16)

        @block.tensor
        def _(pe):
            pe.wait_ge(g_ready, 1)
            flat = lambda a: a.rearrange("p a b -> p (a b)")
            nc.tensor.matmul(c_ps[:, 0:NT * H], cum[:, :], flat(z[:, :, :]), start=True, stop=True).then_inc(summed, 1)
            pe.wait_ge(sum_ready, 1)
            for n, sel in enumerate((last_sel[:, 0, :], last_sel[:, 1, :], own[:, :])):
                last = nc.tensor.matmul(l_ps[n][:, 0:NT * H], sel, flat(tab[:, 0, :, :]), start=True, stop=True)
            last.then_inc(lasts, 1)

        @block.gpsimd
        def _(pool):
            nc.gpsimd.memset(zeros[:, :], 0.0).then_inc(zeroed, 1)
            pool.wait_ge(small, 16 * len(smalls))
            for t in range(NT):
                pool.wait_ge(loaded[t % 2], 16 * CONV * (t // 2 + 1))
                nc.gpsimd.tensor_tensor(x[t % 2][:, 0:2, :], x[t % 2][:, 0:2, :], taps[:, 0:2, :], ALU.mult).then_inc(multiplied, 1)

        @block.scalar
        def _(act):
            chain = g.chain(act)
            act.wait_ge(small, 16 * len(smalls))
            act.wait_ge(to_act, 1)
            chain(nc.scalar.activation(t1[:, :, :], z[:, :, :], ACT.Abs))
            chain(nc.scalar.activation(t1[:, :, :], t1[:, :, :], ACT.Exp, scale=-1.0))
            nc.scalar.activation(alog[:, :], alog[:, :], ACT.Exp)
            chain(nc.scalar.activation(t1[:, :, :], t1[:, :, :], ACT.Ln, bias=1.0))
            nc.scalar.activation(tab[:, 1, :, :], ab[:, :, 0:H], ACT.Sigmoid).then_inc(from_act, 1)
            act.wait_ge(to_act, 2)
            for n in (2, 3, 5, 6):
                last = nc.scalar.activation(tab[:, n, :, :], tab[:, n, :, :], ACT.Exp)
            last.then_inc(from_act, 1)
            for t in range(NT):
                act.wait_ge(convolved, t + 1)
                nc.scalar.activation(qkv[:, t, :], qkv[:, t, :], ACT.Silu).then_inc(silued, 1)
                act.wait_ge(squared, t + 1)
                nc.scalar.activation(stat[:, :], stat[:, :], ACT.Sqrt, bias=g.eps[:, :]).then_inc(rooted, 1)

        @block.vector
        def _(dve):
            chain = g.chain(dve)
            TT, TS = nc.vector.tensor_tensor, nc.vector.tensor_scalar
            bc = lambda a: a[:, :].unsqueeze(1).broadcast_to([P, NT, H])
            dve.wait_ge(small, 16 * len(smalls))
            TT(z[:, :, :], ab[:, :, H:2 * H], bc(dt), ALU.add).then_inc(to_act, 1)
            dve.wait_ge(from_act, 1)
            chain(TS(z[:, :, :], z[:, :, :], 0.0, None, ALU.max))
            chain(TT(z[:, :, :], z[:, :, :], t1[:, :, :], ALU.add))
            chain(TT(z[:, :, :], z[:, :, :], bc(alog), ALU.mult))
            TS(z[:, :, :], z[:, :, :], -1.0, None, ALU.mult).then_inc(g_ready, 1)
            TS(tab[:, 4, :, :], tab[:, 1, :, :], -1.0, None, ALU.mult)
            dve.wait_ge(summed, 1)
            view = lambda ps: ps[:, 0:NT * H].rearrange("p (a b) -> p a b", b=H)
            nc.vector.tensor_copy(tab[:, 0, :, :], view(c_ps)).then_inc(sum_ready, 1)
            dve.wait_ge(sum_ready, 1)
            dve.wait_ge(lasts, 1)
            nc.vector.tensor_copy(tab[:, 2, :, :], tab[:, 0, :, :])
            TT(tab[:, 3, :, :], view(l_ps[2]), tab[:, 0, :, :], ALU.subtract)
            nc.vector.tensor_copy(tab[:, 5, :, :], view(l_ps[0]))
            nc.vector.tensor_copy(tab[:, 6, :, :], view(l_ps[1])).then_inc(to_act, 1)
            for t in range(NT):
                X, Q = x[t % 2], qkv[:, t, :]
                dve.wait_ge(loaded[t % 2], 16 * CONV * (t // 2 + 1))
                chain(TT(X[:, 2:4, :], X[:, 2:4, :], taps[:, 2:4, :], ALU.mult))
                chain(TT(X[:, 2, :], X[:, 2, :], X[:, 3, :], ALU.add))
                dve.wait_ge(multiplied, t + 1)
                chain(TT(X[:, 0, :], X[:, 0, :], X[:, 1, :], ALU.add))
                TT(Q, X[:, 0, :], X[:, 2, :], ALU.add).then_inc(convolved, 1)
                dve.wait_ge(silued, t + 1)
                qk = qkv[:, t, 0:2 * W].rearrange("p (h d) -> p h d", d=DH)
                chain(TT(square[:, :, :], qk, qk, ALU.mult))
                nc.vector.tensor_reduce(stat[:, :], square[:, :, :], AX, ALU.add).then_inc(squared, 1)
                dve.wait_ge(rooted, t + 1)
                chain(nc.vector.reciprocal(stat[:, :], stat[:, :]))
                chain(TS(stat[:, 0:H], stat[:, 0:H], DH ** -0.5, None, ALU.mult))
                TT(qk, qk, stat[:, :].unsqueeze(2).broadcast_to([P, 2 * H, DH]), ALU.mult).then_inc(done, 1)
                dve.wait_ge(done, t + 1)


def delta_scan(nc, g, qkv, tab):
    LEVELS = 5
    with stage(nc, g) as ctx:
        sb = lambda n, shape: ctx.enter_context(nc.sbuf_tensor("ds_" + n, shape, F32))
        wide = [P, H, P]
        strict, incl = sb("strict", [P, P]), sb("incl", [P, P])
        kT, qT, qgT, wT = (sb(n, [DH, H, P]) for n in ("kT", "qT", "qgT", "wT"))
        qg, kd = sb("qg", [P, H, DH]), sb("kd", [P, H, DH])
        rhs, uw = sb("rhs", wide), sb("uw", wide)
        diag, dec, decT, qk = sb("diag", wide), sb("dec", wide), sb("decT", wide), sb("qk", wide)
        M = [sb(f"M{b}", wide) for b in range(2)]
        MT = [sb(f"MT{b}", wide) for b in range(2)]
        TT_ = sb("TT", wide)
        vnew, o1, o = sb("vnew", [P, H, DH]), sb("o1", [P, H, DH]), sb("o", [P, H, DH])
        state = sb("state", [DH, H, DH])
        z = [sb(f"z{b}", [P, H, DH]) for b in range(2)]
        gain, stat = sb("gain", [P, DH]), sb("stat", [P, H])
        ones = sb("ones", [P, P])
        square = sb("square", [P, H, DH])
        y = [sb(f"y{b}", [P, H, DH]) for b in range(2)]
        pA, pB, pC = (ctx.enter_context(nc.psum_tensor("ds_" + n, wide, F32)) for n in "ABC")
        pD = [ctx.enter_context(nc.psum_tensor(f"ds_D{b}", [P, H, DH], F32)) for b in range(2)]
        small = g.sem("ds_small")
        z_loaded = [g.sem(f"ds_z_loaded{b}") for b in range(2)]
        stored = [g.sem(f"ds_stored{b}") for b in range(2)]
        pe_did, act_did, dve_did, pool_did = (g.sem("ds_" + n) for n in ("pe_did", "act_did", "dve_did", "pool_did"))
        PE_STEPS = ["kT", "qT", "qgT", "decay", "kk", "qk", "MT"]
        for l in range(LEVELS):
            PE_STEPS += [f"M{l}", f"MT{l}", f"upd{l}"] if l < LEVELS - 1 else [f"M{l}", f"upd{l}"]
        PE_STEPS += ["sol", "wT"]
        for j in range(2):
            PE_STEPS += [f"wS{j}", f"qS{j}", f"qkv{j}", f"kv{j}"]
        ACT_STEPS = ["kT", "qgT", "dec", "decT", "MT"] + [f"M{l}" for l in range(LEVELS)] + ["uw"]
        for j in range(2):
            ACT_STEPS += [f"qS{j}"]
        ACT_STEPS += ["silu_z", "root"]
        DVE_STEPS = ["rhs", "diag", "kd", "qT", "sub", "M", "qk", "TT"]
        for l in range(LEVELS):
            DVE_STEPS += [f"MT{l}", f"upd{l}"] if l < LEVELS - 1 else [f"upd{l}"]
        DVE_STEPS += ["wT"]
        for j in range(2):
            DVE_STEPS += [f"vnew{j}", f"o{j}", f"state{j}"]
        DVE_STEPS += ["squares", "y"]
        POOL_STEPS = ["qg", "decT"]

        def wait(eng, sem, steps, name, t):
            eng.wait_ge(sem, len(steps) * t + steps.index(name) + 1)
        pe_ = lambda eng, name, t: wait(eng, pe_did, PE_STEPS, name, t)
        act_ = lambda eng, name, t: wait(eng, act_did, ACT_STEPS, name, t)
        dve_ = lambda eng, name, t: wait(eng, dve_did, DVE_STEPS, name, t)
        pool_ = lambda eng, name, t: wait(eng, pool_did, POOL_STEPS, name, t)
        smalls = [(strict[:, :], g.d["c_strict64"]), (incl[:, :], g.d["c_cum64"]), (gain[:, :], row_bcast(g.d["delta_norm_g_2"][0], DH))]
        block = ctx.enter_context(nc.Block())

        def store(sp, t):
            dve_(sp, "y", t)
            sp.dma_start(rows(g.d["y_delta"])[:, t, :], y[t % 2][:, :, :].rearrange("p h d -> p (h d)")).then_inc(stored[t % 2], 16)

        @block.sync
        def _(sp):
            for dst, src in smalls:
                sp.dma_start(dst, src).then_inc(small, 16)
            for t in range(NT):
                if t >= 2:
                    dve_(sp, "y", t - 2)
                sp.dma_start(z[t % 2][:, :, :].rearrange("p h d -> p (h d)"), rows(g.d["proj2"])[:, t, C_Z:C_Z + W]).then_inc(z_loaded[t % 2], 16)
                if t >= 1:
                    store(sp, t - 1)
            store(sp, NT - 1)
            for b in range(2):
                sp.wait_ge(stored[b], 16 * (NT // 2))

        @block.tensor
        def _(pe):
            mm = lambda out, a, b: nc.tensor.matmul(out, a, b, start=True, stop=True)
            did = lambda last: last.then_inc(pe_did, 1)
            pe.wait_ge(small, 16 * len(smalls))
            for t in range(NT):
                head = lambda base, h: qkv[:, t, base + h * DH:base + (h + 1) * DH]
                if t == 0:
                    dve_(pe, "rhs", 0)
                for h in range(H):
                    last = nc.tensor.transpose(pA[0:DH, h, :], head(W, h), g.ident[:, :])
                did(last)
                for h in range(H):
                    last = nc.tensor.transpose(pB[0:DH, h, :], head(0, h), g.ident[:, :])
                did(last)
                pool_(pe, "qg", t)
                if t >= 1:
                    dve_(pe, "state1", t - 1)
                for h in range(H):
                    last = nc.tensor.transpose(pC[0:DH, h, :], qg[:, h, :], g.ident[:, :])
                did(last)
                act_(pe, "kT", t)
                dve_(pe, "diag", t)
                flat = lambda a: a[:, :, :].rearrange("p a b -> p (a b)")
                for c in range(0, H * P, CH):
                    last = mm(flat(pA)[:, c:c + CH], ones[:, :], flat(diag)[:, c:c + CH])
                did(last)
                dve_(pe, "qT", t)
                for h in range(H):
                    last = mm(pB[:, h, :], kT[:, h, :], kT[:, h, :])
                did(last)
                act_(pe, "qgT", t)
                for h in range(H):
                    last = mm(pC[:, h, :], kT[:, h, :], qT[:, h, :])
                did(last)
                dve_(pe, "M", t)
                for h in range(H):
                    last = nc.tensor.transpose(pA[:, h, :], M[0][:, h, :], g.ident[:, :])
                did(last)
                dve_(pe, "qk", t)
                dve_(pe, "TT", t)
                for l in range(LEVELS):
                    a = l % 2
                    for h in range(H):
                        last = mm(pB[:, h, :], MT[a][:, h, :], M[a][:, h, :])
                    did(last)
                    if l < LEVELS - 1:
                        for h in range(H):
                            last = mm(pC[:, h, :], M[a][:, h, :], MT[a][:, h, :])
                        did(last)
                    act_(pe, f"M{l}", t)
                    for h in range(H):
                        last = mm(pA[:, h, :], M[1 - a][:, h, :], TT_[:, h, :])
                    did(last)
                    dve_(pe, f"upd{l}", t)
                for h in range(H):
                    last = mm(pA[:, h, :], TT_[:, h, :], rhs[:, h, :])
                did(last)
                act_(pe, "uw", t)
                for h in range(H):
                    last = nc.tensor.transpose(pB[0:DH, h, :], uw[:, h, DH:P], g.ident[:, :])
                did(last)
                dve_(pe, "wT", t)
                for j in range(2):
                    r = slice(j * CK, (j + 1) * CK)
                    if j == 1:
                        dve_(pe, "state0", t)
                    for h in range(H):
                        last = mm(pD[0][r, h, :], wT[:, h, r], state[:, h, :])
                    did(last)
                    for h in range(H):
                        last = mm(pD[1][r, h, :], qgT[:, h, r], state[:, h, :])
                    did(last)
                    dve_(pe, f"vnew{j}", t)
                    for h in range(H):
                        last = mm(pB[r, h, 0:DH], qk[r, h, r], vnew[r, h, :])
                    did(last)
                    for h in range(H):
                        last = mm(pC[0:DH, h, 0:DH], kd[r, h, :], vnew[r, h, :])
                    did(last)

        @block.gpsimd
        def _(pool):
            pool.wait_ge(small, 16 * len(smalls))
            for t in range(NT):
                if t >= 1:
                    pe_(pool, "qgT", t - 1)
                nc.gpsimd.tensor_tensor(qg[:, :, :], qkv[:, t, 0:W].rearrange("p (h d) -> p h d", d=DH),
                                        tab[:, 2, t, :].unsqueeze(2).broadcast_to([P, H, DH]), ALU.mult).then_inc(pool_did, 1)
                act_(pool, "decT", t)
                nc.gpsimd.tensor_tensor(decT[:, :, :], decT[:, :, :], incl[:, :].unsqueeze(1).broadcast_to(wide), ALU.mult).then_inc(pool_did, 1)

        @block.scalar
        def _(act):
            did = lambda last: last.then_inc(act_did, 1)
            copy = nc.scalar.copy
            for t in range(NT):
                pe_(act, "kT", t)
                did(copy(kT[:, :, :], pA[0:DH, :, :]))
                pe_(act, "qgT", t)
                if t >= 1:
                    pe_(act, "qS1", t - 1)
                did(copy(qgT[:, :, :], pC[0:DH, :, :]))
                dve_(act, "sub", t)
                did(nc.scalar.activation(dec[:, :, :], dec[:, :, :], ACT.Exp, scale=-1.0))
                did(nc.scalar.activation(decT[:, :, :], decT[:, :, :], ACT.Exp))
                pe_(act, "MT", t)
                did(copy(MT[0][:, :, :], pA[:, :, :]))
                for l in range(LEVELS):
                    pe_(act, f"M{l}", t)
                    if l >= 1:
                        pe_(act, f"upd{l - 1}", t)
                    did(copy(M[1 - l % 2][:, :, :], pB[:, :, :]))
                pe_(act, "sol", t)
                did(copy(uw[:, :, :], pA[:, :, :]))
                for j in range(2):
                    r = slice(j * CK, (j + 1) * CK)
                    pe_(act, f"qS{j}", t)
                    did(copy(o1[r, :, :], pD[1][r, :, :]))
                act.wait_ge(z_loaded[t % 2], 16 * (t // 2 + 1))
                did(nc.scalar.activation(z[t % 2][:, :, :], z[t % 2][:, :, :], ACT.Silu))
                dve_(act, "squares", t)
                did(nc.scalar.activation(stat[:, :], stat[:, :], ACT.Sqrt, scale=1.0 / DH, bias=g.eps[:, :]))

        @block.vector
        def _(dve):
            chain = g.chain(dve)
            TT, TS, copy = nc.vector.tensor_tensor, nc.vector.tensor_scalar, nc.vector.tensor_copy
            did = lambda last: last.then_inc(dve_did, 1)
            chain(nc.vector.memset(ones[:, :], 1.0))
            chain(nc.vector.memset(state[:, :, :], 0.0))
            dve.wait_ge(small, 16 * len(smalls))
            for t in range(NT):
                by = lambda n, w: tab[:, n, t, :].unsqueeze(2).broadcast_to([P, H, w])
                over = lambda m: m[:, :].unsqueeze(1).broadcast_to(wide)
                k = qkv[:, t, W:2 * W].rearrange("p (h d) -> p h d", d=DH)
                v = qkv[:, t, 2 * W:3 * W].rearrange("p (h d) -> p h d", d=DH)
                chain(TT(rhs[:, :, 0:DH], v, by(1, DH), ALU.mult))
                chain(TT(rhs[:, :, DH:P], k, by(1, DH), ALU.mult))
                did(TT(rhs[:, :, DH:P], rhs[:, :, DH:P], by(2, DH), ALU.mult))
                did(TT(diag[:, :, :], over(g.ident), by(0, P), ALU.mult))
                did(TT(kd[:, :, :], k, by(3, DH), ALU.mult))
                pe_(dve, "qT", t)
                did(copy(qT[:, :, :], pB[0:DH, :, :]))
                pe_(dve, "decay", t)
                chain(TT(dec[:, :, :], pA[:, :, :], by(0, P), ALU.subtract))
                chain(TS(decT[:, :, :], dec[:, :, :], 0.0, None, ALU.min))
                did(TS(dec[:, :, :], dec[:, :, :], 0.0, None, ALU.max))
                act_(dve, "dec", t)
                chain(TT(dec[:, :, :], dec[:, :, :], over(strict), ALU.mult))
                chain(TT(dec[:, :, :], dec[:, :, :], by(4, P), ALU.mult))
                pe_(dve, "kk", t)
                did(TT(M[0][:, :, :], pB[:, :, :], dec[:, :, :], ALU.mult))
                pe_(dve, "qk", t)
                pool_(dve, "decT", t)
                did(TT(qk[:, :, :], pC[:, :, :], decT[:, :, :], ALU.mult))
                act_(dve, "MT", t)
                did(TT(TT_[:, :, :], MT[0][:, :, :], over(g.ident), ALU.add))
                for l in range(LEVELS):
                    if l < LEVELS - 1:
                        pe_(dve, f"MT{l}", t)
                        did(copy(MT[1 - l % 2][:, :, :], pC[:, :, :]))
                    pe_(dve, f"upd{l}", t)
                    did(TT(TT_[:, :, :], TT_[:, :, :], pA[:, :, :], ALU.add))
                pe_(dve, "wT", t)
                did(copy(wT[:, :, :], pB[0:DH, :, :]))
                for j in range(2):
                    r = slice(j * CK, (j + 1) * CK)
                    pe_(dve, f"wS{j}", t)
                    did(TT(vnew[r, :, :], uw[r, :, 0:DH], pD[0][r, :, :], ALU.subtract))
                    pe_(dve, f"qkv{j}", t)
                    act_(dve, f"qS{j}", t)
                    did(TT(o[r, :, :], o1[r, :, :], pB[r, :, 0:DH], ALU.add))
                    pe_(dve, f"kv{j}", t)
                    chain(TT(state[:, :, :], state[:, :, :], tab[0:DH, 5 + j, t, :].unsqueeze(2).broadcast_to([DH, H, DH]), ALU.mult))
                    did(TT(state[:, :, :], state[:, :, :], pC[0:DH, :, 0:DH], ALU.add))
                dve_(dve, "state1", t)
                chain(TT(square[:, :, :], o[:, :, :], o[:, :, :], ALU.mult))
                did(nc.vector.tensor_reduce(stat[:, :], square[:, :, :], AX, ALU.add))
                act_(dve, "root", t)
                chain(nc.vector.reciprocal(stat[:, :], stat[:, :]))
                chain(TT(o[:, :, :], o[:, :, :], stat[:, :].unsqueeze(2).broadcast_to([P, H, DH]), ALU.mult))
                chain(TT(o[:, :, :], o[:, :, :], gain[:, :].unsqueeze(1).broadcast_to([P, H, DH]), ALU.mult))
                if t >= 2:
                    dve.wait_ge(stored[t % 2], 16 * (t // 2))
                did(TT(y[t % 2][:, :, :], o[:, :, :], z[t % 2][:, :, :], ALU.mult))


def delta(nc, g):
    with ExitStack() as ctx:
        qkv = ctx.enter_context(nc.sbuf_tensor("dt_qkv", [P, NT, 3 * W], F32))
        tab = ctx.enter_context(nc.sbuf_tensor("dt_tab", [P, 7, NT, H], F32))
        delta_prepare(nc, g, qkv, tab)
        delta_scan(nc, g, qkv, tab)


def constants():
    f, i = np.float32, np.arange(P)
    c = {}
    same = i[:, None] // CK == i[None, :] // CK
    c["c_ident"] = np.eye(P, dtype=f)
    c["c_tri"] = (i[:, None] <= i[None, :]).astype(f)
    c["c_tri_strict"] = (i[:, None] < i[None, :]).astype(f)
    c["c_causal"] = np.where(i[None, :] <= i[:, None], 0, NEG).astype(f)
    c["c_pick"] = (NE - np.arange(NE)).astype(f)
    c["c_inv"] = (10000.0 ** (-np.arange(DH // 2) / (DH / 2))).astype(f)
    c["c_cum64"] = (same & (i[:, None] <= i[None, :])).astype(f)
    c["c_strict64"] = (same & (i[:, None] > i[None, :])).astype(f)
    c["c_last"] = np.stack([np.repeat((i == CK - 1)[:, None], P, 1), np.repeat((i == P - 1)[:, None], P, 1),
                            i[:, None] == i[None, :] // CK * CK + CK - 1], 1).astype(f)
    bucket = np.zeros((33, BRANCHES, SPAN), f)
    for r, dil in enumerate((1, 4, 16)):
        for m in range(SPAN):
            steps = 2 * P - 1 - m
            d = steps * dil
            if not 0 <= steps <= P:
                bucket[32, r, m] = 1
            elif d < 16:
                bucket[d, r, m] = 1
            else:
                large = 16 + int(np.log(f(d) / f(16)) / f(np.log(2048 / 16)) * f(16))
                bucket[min(large, 31), r, m] = 1
    c["c_bucket"] = bucket
    return c


def program(nc, d):
    with ExitStack() as ctx:
        scratch = lambda name, shape, dt=F32: nc.dram_tensor(name, shape, dt).ap()
        d["proj1"] = scratch("proj1", (S, N1))
        d["out_fox"], d["out_dsa"] = scratch("out_fox", (S, W)), scratch("out_dsa", (S, W))
        d["merged"], d["x1"], d["x2"] = scratch("merged", (S, D)), scratch("x1", (S, D)), scratch("x2", (S, D))
        d["xn2"] = scratch("xn2", (S, D))
        d["table"] = scratch("table", (TABLE * P, 4), I32)
        d["moe_y"] = scratch("moe_y", (SLOTS + P, D))
        d["proj2_padded"] = scratch("proj2_padded", (CONV - 1 + S, N2))
        d["proj2"] = d["proj2_padded"][CONV - 1:, :]
        d["skew"] = scratch("skew", (BRANCHES, H, P * SPAN))
        d["branch"] = scratch("branch", (BRANCHES, S, H * (DH + 2)))
        d["y_attn"], d["y_delta"] = scratch("y_attn", (S, W)), scratch("y_delta", (S, W))
        d["x3"], d["x4"] = scratch("x3", (S, D)), scratch("x4", (S, D))
        g = shared(nc, ctx, d)
        x = d["x"][0]
        gate = lambda blk, half: 48 * blk + 24 * half + 2 * KD

        @contextmanager
        def transposed(name):
            with nc.sbuf_tensor(name, [P, KD, S], F32) as hT:
                yield hT

        modulation(nc, g)
        with transposed("hT1") as hT:
            normalize(nc, g, "n1", x, 0, 0, hT)
            project(nc, g, "p1", hT, d["w_in"][0], C_GATE, d["proj1"])
            forgetting(nc, g)
            sparse(nc, g, hT)
        with transposed("hT2") as hT:
            transpose_rows(nc, g, "tr1", [d["out_fox"], d["out_dsa"]], hT)
            merge(nc, g, hT)
            transpose_rows(nc, g, "tr2", [d["merged"]], hT)
            project_residual(nc, g, "o1", hT, d["w_out"][0], x, gate(0, 0), d["x1"])
            normalize(nc, g, "n2", d["x1"], 0, 1, hT, d["xn2"])
            route(nc, g, hT)
        experts(nc, g)
        combine(nc, g)
        with transposed("hT3") as hT:
            normalize(nc, g, "n3", d["x2"], 1, 0, hT)
            project(nc, g, "p2", hT, d["w_in_2"][0], N2, d["proj2"])
        dilated(nc, g)
        delta(nc, g)
        with transposed("hT4") as hT:
            transpose_rows(nc, g, "tr3", [d["y_attn"], d["y_delta"]], hT)
            project_residual(nc, g, "o2", hT, d["w_out_2"][0], d["x2"], gate(1, 0), d["x3"])
        with nc.sbuf_tensor("actT", [P, d["w_gate_2"].shape[2] // P, S], F32) as actT:
            with transposed("hT5") as hT:
                normalize(nc, g, "n4", d["x3"], 1, 1, hT)
                feed_forward_up(nc, g, hT, actT)
            project_residual(nc, g, "dn", actT, d["w_down_2"][0], d["x3"], gate(1, 1), d["x4"], width=CH // 2)
        final_norm(nc, g)


INPUTS = ["x", "c", "positions", "ada_w", "ada_b", "norm1_g", "norm2_g", "w_in", "b_fgt", "b_gate", "qn_fox",
          "kn_fox", "qn_dsa", "kn_dsa", "w_proj_fox", "w_proj_dsa", "w_out", "router_w_grp", "router_b_grp",
          "router_w_exp", "router_b_exp", "exp_w1", "exp_w3", "exp_w2", "c_2", "w_ada_2", "b_ada_2",
          "norm_attn_g_2", "w_in_2", "rel_bias_2", "conv_w_2", "a_log_2", "dt_bias_2", "delta_norm_g_2",
          "w_out_2", "norm_ffn_g_2", "w_gate_2", "w_up_2", "w_down_2", "final_norm_g_2"]


def kernel(**inputs):
    import concourse.bacc as bacc
    from concourse.bass_utils import run_bass_kernel_spmd

    nc = bacc.Bacc("TRN2", target_bir_lowering=False, num_devices=1)
    arrays = {name: np.ascontiguousarray(inputs[name]) for name in INPUTS}
    arrays.update(constants())
    aps = {name: nc.dram_tensor(name, a.shape, mybir.dt.from_np(a.dtype), kind="ExternalInput").ap()
           for name, a in arrays.items()}
    out = nc.dram_tensor("out", (1, S, D), F32, kind="ExternalOutput").ap()
    program(nc, {"out": out[0], **aps})
    r = run_bass_kernel_spmd(nc, [arrays], core_ids=[0])
    return r.results[0]["out"]
```
